# Optimizing a Trainium2 kernel written in Bass

```python
import jax
import jax.numpy as jnp
from jax import lax
import numpy as np

D_MODEL = 1024
BATCH = 1
SEQ = 1024
DEPTH = 1

GRID_W = 64
N_MIXERS = 3
HEAD_DIM = 64
D_FF = 4 * D_MODEL
D_PLE = 256
NA_HEADS = D_MODEL // HEAD_DIM
NA_KH_MAX = 8
NA_KW = 16
GQA_HEADS = D_MODEL // HEAD_DIM
GQA_KV_HEADS = GQA_HEADS // 4
GQA_GROUP = GQA_HEADS // GQA_KV_HEADS
Q_BLOCK = 128
ROPE_THETA = 10000.0
ML_HEADS = 8
ML_DV = D_MODEL // ML_HEADS
ML_DQK = ML_DV // 2
ML_CHUNK = 64
N_A = (DEPTH + N_MIXERS - 1) // N_MIXERS
N_B = (DEPTH + N_MIXERS - 2) // N_MIXERS
N_C = DEPTH // N_MIXERS
DN_ALPHA = (2 * DEPTH) ** 0.25
DN_BETA = (8 * DEPTH) ** -0.25
EPS = 1e-6

kernel_name = 'hybrid_natten_gqa_mlstm_encoder'

def layer_norm(x, g, b):
    xf = x.astype(jnp.float32)
    mu = jnp.mean(xf, -1, keepdims=True)
    var = jnp.mean(jnp.square(xf - mu), -1, keepdims=True)
    return ((xf - mu) * lax.rsqrt(var + EPS) * g.astype(jnp.float32) + b.astype(jnp.float32)).astype(x.dtype)

def rms_norm(x, g):
    xf = x.astype(jnp.float32)
    return xf * lax.rsqrt(jnp.mean(jnp.square(xf), -1, keepdims=True) + EPS) * g.astype(jnp.float32)

def neighborhood_attention(x, w_qkv, rpb, w_o):
    bsz, seq, _ = x.shape
    rows = seq // GRID_W
    kh = min(NA_KH_MAX, rows)
    qkv = (x @ w_qkv).reshape(bsz, rows, GRID_W, 3, NA_HEADS, HEAD_DIM)
    q = qkv[:, :, :, 0] * HEAD_DIM ** -0.5
    k = qkv[:, :, :, 1]
    v = qkv[:, :, :, 2]
    col = np.arange(GRID_W)
    c0 = np.clip(col - NA_KW // 2, 0, GRID_W - NA_KW)
    col_in = (col[None, :] >= c0[:, None]) & (col[None, :] < c0[:, None] + NA_KW)
    dc = np.clip(col[None, :] - col[:, None], 1 - NA_KW, NA_KW - 1) + NA_KW - 1

    def row_block(r):
        r0 = jnp.clip(r - kh // 2, 0, rows - kh)
        q_r = lax.dynamic_index_in_dim(q, r, axis=1, keepdims=False)
        k_b = lax.dynamic_slice_in_dim(k, r0, kh, axis=1)
        v_b = lax.dynamic_slice_in_dim(v, r0, kh, axis=1)
        s = jnp.einsum('bqhd,bakhd->bhqak', q_r, k_b, preferred_element_type=jnp.float32)
        dr = r0 + jnp.arange(kh) - r + NA_KH_MAX - 1
        bias = rpb[:, dr[None, :, None], dc[:, None, :]].astype(jnp.float32)
        s = jnp.where(col_in[:, None, :], s + bias, -jnp.inf)
        pr = jax.nn.softmax(s, axis=(-2, -1))
        return jnp.einsum('bhqak,bakhd->bqhd', pr.astype(v.dtype), v_b)

    out = lax.map(row_block, jnp.arange(rows))
    return jnp.moveaxis(out, 0, 1).reshape(bsz, seq, D_MODEL) @ w_o

def axial_rope_tables(seq):
    t = jnp.arange(seq)
    row = (t // GRID_W).astype(jnp.float32)
    col = (t % GRID_W).astype(jnp.float32)
    n_pairs = HEAD_DIM // 4
    inv = ROPE_THETA ** (-jnp.arange(n_pairs, dtype=jnp.float32) / n_pairs)
    ang = jnp.concatenate([row[:, None] * inv, col[:, None] * inv], -1)
    return jnp.cos(ang), jnp.sin(ang)

def apply_rope(x, cos, sin):
    shape = (x.shape[1],) + (1,) * (x.ndim - 3) + (cos.shape[-1],)
    c = cos.reshape(shape)
    s = sin.reshape(shape)
    x0, x1 = x[..., 0::2], x[..., 1::2]
    return jnp.stack([x0 * c - x1 * s, x0 * s + x1 * c], -1).reshape(x.shape)

def gqa_axial(x, w_qkv, q_norm, k_norm, w_o):
    bsz, seq, _ = x.shape
    kvd = GQA_KV_HEADS * HEAD_DIM
    qkv = x @ w_qkv
    q = qkv[..., :D_MODEL].reshape(bsz, seq, GQA_KV_HEADS, GQA_GROUP, HEAD_DIM)
    k = qkv[..., D_MODEL:D_MODEL + kvd].reshape(bsz, seq, GQA_KV_HEADS, HEAD_DIM)
    v = qkv[..., D_MODEL + kvd:].reshape(bsz, seq, GQA_KV_HEADS, HEAD_DIM)
    cos, sin = axial_rope_tables(seq)
    q = (apply_rope(rms_norm(q, q_norm), cos, sin) * HEAD_DIM ** -0.5).astype(x.dtype)
    k = apply_rope(rms_norm(k, k_norm), cos, sin).astype(x.dtype)
    n_blk = seq // Q_BLOCK
    qb = jnp.moveaxis(q.reshape(bsz, n_blk, Q_BLOCK, GQA_KV_HEADS, GQA_GROUP, HEAD_DIM), 1, 0)

    def block(q_blk):
        s = jnp.einsum('bqkgd,bskd->bkgqs', q_blk, k, preferred_element_type=jnp.float32)
        pr = jax.nn.softmax(s, axis=-1)
        return jnp.einsum('bkgqs,bskd->bqkgd', pr.astype(v.dtype), v)

    out = lax.map(block, qb)
    return jnp.moveaxis(out, 0, 1).reshape(bsz, seq, D_MODEL) @ w_o

def mlstm_scan(q, k, v, log_i, log_f):
    bsz, nh, seq, dqk = q.shape
    dv = v.shape[-1]
    nc, L = seq // ML_CHUNK, ML_CHUNK
    qc, kc, vc = [jnp.moveaxis(a.reshape(bsz, nh, nc, L, a.shape[-1]), 2, 0) for a in (q, k, v)]
    ic, fc = [jnp.moveaxis(a.reshape(bsz, nh, nc, L), 2, 0) for a in (log_i, log_f)]
    tri = jnp.tril(jnp.ones((L, L), bool))

    def step(carry, xs):
        C, n, m = carry
        q_, k_, v_, li, lf = xs
        b = jnp.cumsum(lf, axis=-1)
        d = jnp.where(tri, b[..., :, None] - b[..., None, :] + li[..., None, :], -jnp.inf)
        inter = b + m[..., None]
        m_t = jnp.maximum(jnp.max(d, -1), inter)
        w = jnp.exp(d - m_t[..., None])
        s_inter = jnp.exp(inter - m_t)
        qk = jnp.einsum('bhtd,bhsd->bhts', q_, k_) * w
        num = s_inter[..., None] * jnp.einsum('bhtd,bhdv->bhtv', q_, C) + jnp.einsum('bhts,bhsv->bhtv', qk, v_)
        den = s_inter * jnp.einsum('bhtd,bhd->bht', q_, n) + jnp.sum(qk, -1)
        h = num / jnp.maximum(jnp.abs(den), jnp.exp(-m_t))[..., None]
        b_last = b[..., -1]
        g = b_last[..., None] - b + li
        m_new = jnp.maximum(b_last + m, jnp.max(g, -1))
        decay = jnp.exp(b_last + m - m_new)
        wk = jnp.exp(g - m_new[..., None])[..., None] * k_
        C_new = decay[..., None, None] * C + jnp.einsum('bhsd,bhsv->bhdv', wk, v_)
        n_new = decay[..., None] * n + jnp.sum(wk, -2)
        return (C_new, n_new, m_new), h

    init = (jnp.zeros((bsz, nh, dqk, dv), jnp.float32), jnp.zeros((bsz, nh, dqk), jnp.float32),
            jnp.zeros((bsz, nh), jnp.float32))
    _, h = lax.scan(step, init, (qc, kc, vc, ic, fc))
    return jnp.moveaxis(h, 0, 2).reshape(bsz, nh, seq, dv)

def mlstm_mixer(x, w_in, b_gates, norm_g, w_o):
    bsz, seq, _ = x.shape
    qk_w = ML_HEADS * ML_DQK
    z = x @ w_in

    def heads(a, dh):
        return a.reshape(bsz, seq, ML_HEADS, dh).transpose(0, 2, 1, 3).astype(jnp.float32)

    q = heads(z[..., :qk_w], ML_DQK) * ML_DQK ** -0.5
    k = heads(z[..., qk_w:2 * qk_w], ML_DQK)
    v = heads(z[..., 2 * qk_w:2 * qk_w + D_MODEL], ML_DV)
    o = jax.nn.sigmoid(z[..., 2 * qk_w + D_MODEL:2 * qk_w + 2 * D_MODEL].astype(jnp.float32))
    gates = (z[..., 2 * qk_w + 2 * D_MODEL:].astype(jnp.float32) + b_gates.astype(jnp.float32))
    gates = gates.reshape(bsz, seq, 4, ML_HEADS).transpose(2, 0, 3, 1)
    i_fw, f_fw, i_bw, f_bw = gates[0], gates[1], gates[2], gates[3]
    h_fw = mlstm_scan(q, k, v, i_fw, jax.nn.log_sigmoid(f_fw))
    flip = lambda a: jnp.flip(a, axis=2)
    h_bw = flip(mlstm_scan(flip(q), flip(k), flip(v), flip(i_bw), flip(jax.nn.log_sigmoid(f_bw))))
    h = (h_fw + h_bw).transpose(0, 2, 1, 3)
    h = rms_norm(h, norm_g.reshape(ML_HEADS, ML_DV)).reshape(bsz, seq, D_MODEL)
    return (o * h).astype(x.dtype) @ w_o

def setup_inputs(seed: int = 0) -> dict:
    key = jax.random.key(seed)
    ks = jax.random.split(key, 24)
    f32 = jnp.float32

    def dense(k, shape, scale=1.0):
        return jax.random.normal(k, shape, f32) * (shape[-2] ** -0.5) * scale

    def gain(k, shape):
        return 1.0 + 0.02 * jax.random.normal(k, shape, f32)

    def small(k, shape):
        return 0.02 * jax.random.normal(k, shape, f32)

    x = jax.random.normal(ks[0], (BATCH, SEQ, D_MODEL), f32)
    p = jax.random.normal(ks[1], (DEPTH, BATCH, SEQ, D_PLE), f32)
    na_scale = jnp.concatenate([jnp.ones((2 * D_MODEL,), f32), jnp.full((D_MODEL,), DN_BETA, f32)])
    na_w_qkv = dense(ks[2], (N_A, D_MODEL, 3 * D_MODEL)) * na_scale
    na_rpb = small(ks[3], (N_A, NA_HEADS, 2 * NA_KH_MAX - 1, 2 * NA_KW - 1))
    na_w_o = dense(ks[4], (N_A, D_MODEL, D_MODEL), DN_BETA)
    kvd = GQA_KV_HEADS * HEAD_DIM
    gq_scale = jnp.concatenate([jnp.ones((D_MODEL + kvd,), f32), jnp.full((kvd,), DN_BETA, f32)])
    gq_w_qkv = dense(ks[5], (N_B, D_MODEL, D_MODEL + 2 * kvd)) * gq_scale
    gq_q_norm = gain(ks[6], (N_B, HEAD_DIM))
    gq_k_norm = gain(ks[7], (N_B, HEAD_DIM))
    gq_w_o = dense(ks[8], (N_B, D_MODEL, D_MODEL), DN_BETA)
    ml_cols = 2 * ML_HEADS * ML_DQK + 2 * D_MODEL + 4 * ML_HEADS
    ml_w_in = dense(ks[9], (N_C, D_MODEL, ml_cols))
    f_bias = jnp.linspace(3.0, 6.0, ML_HEADS, dtype=f32)
    zero_b = jnp.zeros((ML_HEADS,), f32)
    ml_b_gates = (0.1 * jax.random.normal(ks[10], (N_C, 4, ML_HEADS), f32)
                  + jnp.stack([zero_b, f_bias, zero_b, f_bias])).reshape(N_C, 4 * ML_HEADS)
    ml_norm_g = gain(ks[11], (N_C, D_MODEL))
    ml_w_o = dense(ks[12], (N_C, D_MODEL, D_MODEL), DN_BETA)
    ln1_g = gain(ks[13], (DEPTH, D_MODEL))
    ln1_b = small(ks[14], (DEPTH, D_MODEL))
    w_ff1 = dense(ks[15], (DEPTH, D_MODEL, D_FF))
    w_ff2 = dense(ks[16], (DEPTH, D_FF, D_MODEL), DN_BETA)
    ln2_g = gain(ks[17], (DEPTH, D_MODEL))
    ln2_b = small(ks[18], (DEPTH, D_MODEL))
    w_ple_gate = dense(ks[19], (DEPTH, D_MODEL, D_MODEL))
    w_ple_proj = dense(ks[20], (DEPTH, D_PLE, D_MODEL), DN_BETA)
    return {'x': x, 'p': p, 'na_w_qkv': na_w_qkv, 'na_rpb': na_rpb, 'na_w_o': na_w_o,
            'gq_w_qkv': gq_w_qkv, 'gq_q_norm': gq_q_norm, 'gq_k_norm': gq_k_norm, 'gq_w_o': gq_w_o,
            'ml_w_in': ml_w_in, 'ml_b_gates': ml_b_gates, 'ml_norm_g': ml_norm_g, 'ml_w_o': ml_w_o,
            'ln1_g': ln1_g, 'ln1_b': ln1_b, 'w_ff1': w_ff1, 'w_ff2': w_ff2, 'ln2_g': ln2_g, 'ln2_b': ln2_b,
            'w_ple_gate': w_ple_gate, 'w_ple_proj': w_ple_proj}

def reference(x, p, na_w_qkv, na_rpb, na_w_o, gq_w_qkv, gq_q_norm, gq_k_norm, gq_w_o,
              ml_w_in, ml_b_gates, ml_norm_g, ml_w_o, ln1_g, ln1_b, w_ff1, w_ff2, ln2_g, ln2_b,
              w_ple_gate, w_ple_proj):
    for i in range(DEPTH):
        kind, j = i % N_MIXERS, i // N_MIXERS
        if kind == 0:
            mix = neighborhood_attention(x, na_w_qkv[j], na_rpb[j], na_w_o[j])
        elif kind == 1:
            mix = gqa_axial(x, gq_w_qkv[j], gq_q_norm[j], gq_k_norm[j], gq_w_o[j])
        else:
            mix = mlstm_mixer(x, ml_w_in[j], ml_b_gates[j], ml_norm_g[j], ml_w_o[j])
        x = layer_norm(DN_ALPHA * x + mix, ln1_g[i], ln1_b[i])
        hid = jnp.square(jax.nn.relu(x @ w_ff1[i]))
        ple = jax.nn.sigmoid(x @ w_ple_gate[i]) * (p[i] @ w_ple_proj[i])
        x = layer_norm(DN_ALPHA * x + hid @ w_ff2[i] + ple, ln2_g[i], ln2_b[i])
    return x


_drawn_inputs = setup_inputs


def setup_inputs(seed=0):
    import zlib

    import numpy as np

    out = dict(_drawn_inputs(seed))
    spreads = {}
    factors = {'na_rpb': 62.8, 'ln1_g': 2.682, 'ln1_b': 2.821, 'ln2_g': 8.236, 'ln2_b': 8.345}
    for name, (base, spread) in spreads.items():
        noise = np.random.default_rng([zlib.crc32(name.encode()), seed]).standard_normal(out[name].shape)
        drawn = base * np.exp(spread * noise) if base else spread * noise
        out[name] = jnp.asarray(drawn.astype(out[name].dtype))
    for name, factor in factors.items():
        out[name] = (out[name] * factor).astype(out[name].dtype)
    return out
```

```python
from contextlib import ExitStack

import numpy as np

import concourse.bass as bass
from concourse import mybir

P = 128
D = 1024
T = 1024
HEAD = 64
HEADS = D // HEAD
PAIRS = HEADS // 2
GRID_W = 64
ROWS = T // GRID_W
KH, KW = 8, 16
GC = 8
GROUPS = T // P
KC = D // P
HALF = 512
DR, DC = 2 * KH - 1, 2 * KW - 1
NB = 3 * P
FF = 4 * D
PLE = 256
ALPHA = float(2 ** 0.25)
EPS = 1e-6
MASKED = -1e38

F32 = mybir.dt.float32
F32R = mybir.dt.float32r
ALU = mybir.AluOpType
ACT = mybir.ActivationFunctionType

V_, K_, Q_ = range(3)
W_COLUMN = {V_: 2 * D, K_: D, Q_: 0}
PASSES = ((0, 0), (0, 1), (1, 0))

UNITS = 2 * GROUPS
STEPS = UNITS + 4
GROUP_MMS = KC * len(PASSES)
FILL = 6 * GROUP_MMS
FILL_STEPS = STEPS - 1
EVAC_STEP = [(GROUP_MMS * (gi + 1) - 1) * FILL_STEPS // FILL + 1 for gi in range(6)]
V_TILE_STEP = (6, 9)


def transposed_tiles(with_v):
    out = []
    for s in range(STEPS):
        if 2 <= s < UNITS + 2:
            out.append((s, "P", s - 2))
        if with_v and s in V_TILE_STEP:
            out.append((s, "V", V_TILE_STEP.index(s)))
    return out


N_TILES = len(transposed_tiles(True))


def tiles_at(step, with_v):
    return [(n, kind, i) for n, (s, kind, i) in enumerate(transposed_tiles(with_v)) if s == step]


def blocks_of(g):
    return [d for d in (-1, 0, 1) if 0 <= g + d < GROUPS]


def runs_of(g):
    out = []
    for d in blocks_of(g):
        if out and (g + d) % 4:
            out[-1][1] += 1
        else:
            out.append([d, 1])
    return out


def pv_units_at(s):
    out = []
    for h in range(2):
        for k in range(GROUPS):
            if s == GROUPS * h + min(k + 1, GROUPS - 1) + 4:
                out.append((h, k))
    return out


def out_evac_at(s):
    return [(h, b) for h in range(2) for b in range(2) if s == GROUPS * h + (10 if b == 0 else 12)]


class Shared:
    pass


def build_program(nc, x, p, w_qkv, rpb, w_o, ln1_g, ln1_b, w_ff1, w_ff2, ln2_g, ln2_b, w_gate, w_proj, mask, out):
    with ExitStack() as ctx:
        S = Shared()
        S.raw = ctx.enter_context(nc.sbuf_tensor("weight_raw", [P, 4, D], F32))
        S.ident = ctx.enter_context(nc.sbuf_tensor("identity", [P, P], F32))
        S.act = [ctx.enter_context(nc.sbuf_tensor(f"act_T_{n}", [P, KC, T], F32R)) for n in ("hi", "lo")]
        S.ps = [ctx.enter_context(nc.psum_tensor(f"bank{i}", [P, HALF], F32)) for i in range(8)]
        S.oT = nc.dram_tensor("attention_T", [PAIRS, P, T], F32).ap()
        S.rpb_rows = nc.dram_tensor("rpb_rows", [GC, HEADS, DR, 3 * GC], F32).ap()
        S.rpb_stored = ctx.enter_context(nc.semaphore("rpb_rows_stored"))
        S.raw_in, S.wo_in, S.ff_in = ([ctx.enter_context(nc.semaphore(f"{n}_raw_in{i}")) for i in range(4)]
                                      for n in ("qkv", "w_o", "mlp"))
        S.x1 = nc.dram_tensor("x_after_attention", [GROUPS, P, D], F32).ap()
        transpose_input(nc, S, x, w_qkv, rpb)
        attention(nc, S, w_qkv, mask, w_o)
        output_projection(nc, S, x, w_o, ln1_g, ln1_b, p, w_proj)
        mlp(nc, S, p, w_ff1, w_ff2, ln2_g, ln2_b, w_gate, w_proj, out)


def in_register(engine, v):
    return v if isinstance(v, int) else engine.snap(v)


def qkv_chunk(w_qkv, kind, offset):
    return bass.AP(w_qkv.tensor, w_qkv.offset + W_COLUMN[kind] + offset, [[3 * D, P], [P * 3 * D, KC], [1, P]])


def transpose_input(nc, S, x, w_qkv, rpb):
    with ExitStack() as ctx:
        xin = ctx.enter_context(nc.sbuf_tensor("x_tokens", [P, GROUPS, D], F32))
        x_in = [ctx.enter_context(nc.semaphore(f"x_in{g}")) for g in range(GROUPS)]
        zeroed = ctx.enter_context(nc.semaphore("identity_zeroed"))
        ident_ready = ctx.enter_context(nc.semaphore("identity_ready"))
        turned = ctx.enter_context(nc.semaphore("x_turned"))
        hi_done = ctx.enter_context(nc.semaphore("x_hi_done"))
        lo_done = ctx.enter_context(nc.semaphore("x_lo_done"))
        tiles = [(g, q) for g in range(GROUPS) for q in range(2)]
        block = ctx.enter_context(nc.Block())

        @block.sync
        def _(sp):
            for g in range(GROUPS):
                sp.dma_start(xin[:, g, :], token_tile(x, g)).then_inc(x_in[g], 16)
                if g in (1, 3, 5):
                    kind = g // 2
                    sp.dma_start(S.raw[:, kind, :].rearrange("p (k n) -> p k n", k=KC),
                                 qkv_chunk(w_qkv, kind, 0)).then_inc(S.raw_in[kind], 16)

        @block.gpsimd
        def _(pool):
            for c in range(GC):
                src = bass.AP(rpb.tensor, rpb.offset + KW - 1 - GC - c, [[DC, HEADS * DR], [1, 3 * GC]])
                pool.dma_start(S.rpb_rows[c].rearrange("h r w -> (h r) w"), src).then_inc(S.rpb_stored, 16)
            nc.gpsimd.memset(S.ident[:, :], 0.0).then_inc(zeroed, 1)
            pool.wait_ge(zeroed, 1)
            nc.gpsimd.affine_select(out=S.ident[:, :], in_=S.ident[:, :], compare_op=ALU.not_equal, fill=1.0,
                                    base=0, pattern=[[-1, P]], channel_multiplier=1).then_inc(ident_ready, 1)

        @block.tensor
        def _(pe):
            pe.wait_ge(ident_ready, 1)
            for n, (g, q) in enumerate(tiles):
                pe.wait_ge(x_in[g], 16)
                if n >= 8:
                    pe.wait_ge(lo_done, n - 7)
                for i in range(4):
                    k = 4 * q + i
                    last = nc.tensor.transpose(S.ps[n % 8][:, i * P:(i + 1) * P], xin[:, g, k * P:(k + 1) * P],
                                               S.ident[:, :])
                last.then_inc(turned, 1)

        def dest(part, g, q):
            return S.act[part][:, 4 * q:4 * q + 4, g * P:(g + 1) * P]

        def tile(n):
            return S.ps[n % 8][:, :].rearrange("p (i t) -> p i t", i=4)

        @block.scalar
        def _(act):
            for n, (g, q) in enumerate(tiles):
                act.wait_ge(turned, n + 1)
                nc.scalar.activation(dest(0, g, q), tile(n), ACT.Copy).then_inc(hi_done, 1)

        @block.vector
        def _(dve):
            for n, (g, q) in enumerate(tiles):
                dve.wait_ge(hi_done, n + 1)
                nc.vector.tensor_tensor(dest(1, g, q), tile(n), dest(0, g, q).bitcast(F32),
                                        ALU.subtract).then_inc(lo_done, 1)


def token_tile(a, g):
    width = a.shape[-1]
    return bass.AP(a.tensor, a.offset + g * GC * width, [[GRID_W * width, ROWS], [width, GC], [1, width]])


def attention(nc, S, w_qkv, mask, w_o):
    with ExitStack() as ctx:
        def sb(name, shape, dt=F32):
            return ctx.enter_context(nc.sbuf_tensor(name, shape, dt))

        def sem(name):
            return ctx.enter_context(nc.semaphore(name))

        w = [sb(f"w_{n}", [P, 2, KC, P], F32R) for n in ("hi", "lo")]
        q_st = sb("q_hi_lo", [P, 2, 2, T], F32R)
        k_st = [sb(f"k_{n}_twice", [P, 2, 2, T], F32R) for n in ("hi", "lo")]
        v_T = sb("v_T", [P, T])
        v_cat = sb("v_hi_lo", [P, 2, GROUPS, 2, 2, HEAD], F32R)
        bias_in = sb("bias_in", [P, 2, ROWS, 3 * GC])
        bias_inner = sb("bias_inner", [P, 2, NB])
        bias_full = sb("bias_full", [P, 2, NB])
        col_mask = sb("column_mask", [P, NB])
        score = sb("negated_scores", [P, 2, NB])
        nmax = sb("negated_max", [P, 4])
        total = sb("exp_total", [P, 4])
        recip = sb("total_reciprocal", [P, 4])
        spare = sb("spare", [P, 1])
        prob = sb("probabilities", [P, 4, NB])
        pT = [sb(f"prob_T_{n}", [P, 4, NB], F32R) for n in ("hi", "lo")]
        o_low = sb("out_low_part", [P, 2, HALF])
        o_st = sb("out_T", [P, T])

        w_hi = sem("w_hi_done")
        w_lo = sem("w_lo_done")
        proj_full = sem("proj_full")
        proj_free = sem("proj_free")
        proj_hi = sem("proj_hi_done")
        k_ready = sem("k_ready")
        bias_loaded = [sem(f"bias_loaded{h}") for h in range(2)]
        mask_loaded = sem("mask_loaded")
        bias_reset = sem("bias_reset")
        bias_ready = sem("bias_ready")
        score_full = sem("score_full")
        score_done = sem("score_done")
        exp_done = sem("exp_done")
        recip_done = sem("recip_done")
        prob_ready = sem("prob_ready")
        turned = sem("tile_turned")
        turned_hi = sem("tile_hi_done")
        turned_lo = sem("tile_lo_done")
        pv_done = sem("pv_done")
        low_done = sem("out_low_done")
        out_done = sem("out_done")
        out_stored = sem("out_stored")
        block = ctx.enter_context(nc.Block())

        proj_ps, score_ps, tile_ps, out_ps = S.ps[0:2], S.ps[2:4], S.ps[4:6], S.ps[6:8]
        PRE_TILES = 2
        Q_SCALE = HEAD ** -0.5

        def pT_part(buf, g, first, count):
            slot = (g + first) % 4
            base = buf[:, slot, (1 - first) * P:(2 - first) * P]
            return bass.AP(base.tensor, base.offset, [list(base.ap[0]), [NB - P, count], [1, P]])

        def pairs_loop(eng, body):
            with eng.Fori(0, PAIRS // 2 - 1) as it:
                for par in range(2):
                    body(2 * it + par, par, True, True)
            body(PAIRS - 2, 0, True, False)
            body(PAIRS - 1, 1, False, False)

        @block.sync
        def _(sp):
            def value(v):
                return in_register(sp, v)

            def load_w(kind, offset):
                sp.dma_start(S.raw[:, kind, :].rearrange("p (k n) -> p k n", k=KC),
                             qkv_chunk(w_qkv, kind, offset)).then_inc(S.raw_in[kind], 16)

            def load_bias(h, offset, built):
                built = value(built)
                for qr in range(ROWS):
                    r0 = min(max(qr - KH // 2, 0), ROWS - KH)
                    start = value(offset + (r0 - qr + KH - 1) * 3 * GC)
                    if qr == 0:
                        sp.wait_ge(bias_ready, built)
                    src = bass.AP(S.rpb_rows.tensor, start, [[HEADS * DR * 3 * GC, GC], [1, KH * 3 * GC]])
                    sp.dma_start(bias_in[qr * GC:(qr + 1) * GC, h, r0:r0 + KH, :].rearrange("p r w -> p (r w)"), src)\
                      .then_inc(bias_loaded[h], 16)

            sp.sem_inc(out_stored, 16)
            sp.dma_start(col_mask[:, :], mask).then_inc(mask_loaded, 16)
            sp.wait_ge(bias_reset, 1)
            sp.wait_ge(S.rpb_stored, 16 * GC)
            sp.sem_inc(bias_ready, 2)
            for h in range(2):
                load_bias(h, h * DR * 3 * GC, 2)
            for kind in range(3):
                sp.wait_ge(w_hi, kind + 1)
                sp.wait_ge(w_lo, kind + 1)
                load_w(kind, P)
            for h in range(2):
                load_bias(h, (2 + h) * DR * 3 * GC, h + 1 + 2)

            def body(j, par, more, loads):
                if loads:
                    column = value(j * P + 2 * P)
                    for kind in range(3):
                        split = value(3 * j + (3 + kind + 1))
                        sp.wait_ge(w_hi, split)
                        sp.wait_ge(w_lo, split)
                        load_w(kind, column)
                    for h in range(2):
                        load_bias(h, j * (2 * DR * 3 * GC) + (4 + h) * DR * 3 * GC, 2 * j + (2 + h + 1 + 2))
                place, summed = value(j * (P * T)), value(4 * j + (4 + 2))
                sp.wait_ge(out_done, summed)
                sp.dma_start(bass.AP(S.oT.tensor, place, [[T, P], [1, T]]), o_st[:, :]).then_inc(out_stored, 16)

            pairs_loop(sp, body)
            sp.wait_ge(w_lo, 3 * PAIRS)
            for n in range(4):
                load_rows(sp, S, n, w_o, n * P).then_inc(S.wo_in[n], 16)
            sp.wait_ge(out_stored, 16 * (PAIRS + 1))

        @block.gpsimd
        def _(pool):
            nc.gpsimd.memset(bias_in[:, :, :, :], MASKED).then_inc(bias_reset, 1)
            pool.wait_ge(mask_loaded, 16)

            def split(slot, kind, count):
                pool.wait_ge(w_hi, count)
                nc.gpsimd.tensor_tensor(w[1][:, slot, :, :], S.raw[:, kind, :].rearrange("p (k n) -> p k n", k=KC),
                                        w[0][:, slot, :, :].bitcast(F32), ALU.subtract).then_inc(w_lo, 1)

            def build_bias(h, loads):
                pool.wait_ge(bias_loaded[h], loads)
                src = bias_in[:, h, :, :].rearrange("p r (d c) -> p d r c", d=3)
                shape = dict(d=3, r=ROWS)
                nc.gpsimd.tensor_tensor(bias_inner[:, h, :].rearrange("p (d r c) -> p d r c", **shape), src,
                                        col_mask[:, :].rearrange("p (d r c) -> p d r c", **shape), ALU.add)
                nc.gpsimd.tensor_copy(bias_full[:, h, :].rearrange("p (d r c) -> p d r c", **shape), src)\
                    .then_inc(bias_ready, 1)

            split(0, V_, 1)
            split(1, K_, 2)
            for h in range(2):
                build_bias(h, 16 * ROWS)
            split(0, Q_, 3)
            split(1, V_, 4)

            def body(j, par, more, loads):
                if more:
                    split((par + 1 + K_) % 2, K_, 3 * j + (3 + K_ + 1))
                    split((par + 1 + Q_) % 2, Q_, 3 * j + (3 + Q_ + 1))
                    pool.wait_ge(score_done, UNITS * j + (GROUPS + 2))
                    build_bias(0, 16 * ROWS * j + 2 * 16 * ROWS)
                if loads:
                    split(par % 2, V_, 3 * j + (6 + V_ + 1))
                if more:
                    pool.wait_ge(score_done, UNITS * j + (UNITS + 2))
                    build_bias(1, 16 * ROWS * j + 2 * 16 * ROWS)

            pairs_loop(pool, body)

        @block.scalar
        def _(act):
            def split(slot, kind, loads):
                act.wait_ge(S.raw_in[kind], loads)
                nc.scalar.activation(w[0][:, slot, :, :], S.raw[:, kind, :].rearrange("p (k n) -> p k n", k=KC),
                                     ACT.Copy).then_inc(w_hi, 1)

            def evac(par, jn, gi):
                kind, t = gi // 2, gi % 2
                if kind == V_:
                    return
                act.wait_ge(proj_full, 6 * jn + (gi + 1))
                dst = q_st if kind == Q_ else k_st[0]
                for h in range(2):
                    rows = slice(HEAD * h, HEAD * (h + 1))
                    nc.scalar.activation(dst[rows, par, h, t * HALF:(t + 1) * HALF], proj_ps[gi % 2][rows, :],
                                         ACT.Copy, scale=Q_SCALE if kind == Q_ else 1.0).then_inc(proj_hi, 1)

            def turned_tile(par, j, n, kind, index):
                src = tile_ps[n % 2]
                act.wait_ge(turned, N_TILES * j + (PRE_TILES + n + 1))
                if kind == "V":
                    last = nc.scalar.activation(
                        v_cat[:, par, 4 * index:4 * index + 4, :, 0, :],
                        src[:, :].rearrange("p (g h d) -> p g h d", g=4, h=2), ACT.Copy)
                else:
                    g = index % GROUPS
                    act.wait_ge(pv_done, UNITS * j + (index + 1))
                    for first, count in runs_of(g):
                        at = first - blocks_of(g)[0]
                        last = nc.scalar.activation(pT_part(pT[0], g, first, count),
                                                    src[:, at * P:(at + count) * P].rearrange(
                                                        "p (b q) -> p b q", b=count), ACT.Copy)
                last.then_inc(turned_hi, 1)

            def softmax_exp(j, u):
                g = u % GROUPS
                n = P * len(blocks_of(g))
                act.wait_ge(score_done, UNITS * j + (u + 1 + 2))
                nc.scalar.activation(prob[:, u % 4, 0:n], score[:, u % 2, 0:n], ACT.Exp, scale=-1.0,
                                     bias=nmax[:, u % 4:u % 4 + 1],
                                     accum_out=total[:, u % 4:u % 4 + 1]).then_inc(exp_done, 1)

            def out_low(j, h, b):
                act.wait_ge(pv_done, UNITS * j + (GROUPS * h + (5 if b == 0 else 8) + 3))
                act.wait_ge(out_done, 4 * j + (2 * h + b + 1))
                nc.scalar.activation(o_low[0:HEAD, b, :], out_ps[b][HEAD:P, :], ACT.Copy).then_inc(low_done, 1)

            act.sem_inc(exp_done, 2)
            split(0, V_, 16)
            split(1, K_, 16)
            act.wait_ge(proj_full, 2)
            split(0, Q_, 16)
            for t in range(2):
                turned_tile(0, -1, N_TILES - PRE_TILES + t, "V", t)
            for gi in (2, 3):
                evac(0, 0, gi)
            split(1, V_, 32)
            for gi in (4, 5):
                evac(0, 0, gi)

            def body(j, par, more, loads):
                for s in range(STEPS + 1):
                    if more:
                        if s in EVAC_STEP:
                            evac(1 - par, j + 1, EVAC_STEP.index(s))
                        if s == 2:
                            split((par + 1 + K_) % 2, K_, 16 * j + 32)
                        if s == EVAC_STEP[1]:
                            act.wait_ge(proj_full, 6 * j + (6 + 2))
                            split((par + 1 + Q_) % 2, Q_, 16 * j + 32)
                        if loads and s == EVAC_STEP[3] + 1:
                            act.wait_ge(proj_full, 6 * j + (6 + 4))
                            split(par % 2, V_, 16 * j + 48)
                    if s < UNITS:
                        softmax_exp(j, s)
                    for n, kind, index in tiles_at(s - 1, more):
                        turned_tile(1 - par, j, n, kind, index)
                    for h, b in out_evac_at(s):
                        out_low(j, h, b)

            pairs_loop(act, body)

        @block.vector
        def _(dve):
            def evac(par, jn, gi):
                kind, t = gi // 2, gi % 2
                cols = slice(t * HALF, (t + 1) * HALF)
                src = proj_ps[gi % 2]
                if kind == V_:
                    dve.wait_ge(proj_full, 6 * jn + (gi + 1))
                    nc.vector.tensor_copy(v_T[:, cols], src[:, :]).then_inc(proj_free, 1)
                    return
                dve.wait_ge(proj_hi, 8 * jn + (2 * (gi - 2) + 2))
                low, high = slice(0, HEAD), slice(HEAD, P)
                if kind == Q_:
                    for own, other, h in ((low, high, 0), (high, low, 1)):
                        last = nc.vector.scalar_tensor_tensor(
                            out=q_st[other, par, h, cols], in0=src[own, :], scalar=Q_SCALE,
                            in1=q_st[own, par, h, cols].bitcast(F32), op0=ALU.mult, op1=ALU.subtract)
                    last.then_inc(proj_free, 1)
                    return
                for own, h in ((low, 0), (high, 1)):
                    last = nc.vector.tensor_tensor(k_st[1][own, par, h, cols], src[own, :],
                                                   k_st[0][own, par, h, cols].bitcast(F32), ALU.subtract)
                last.then_inc(proj_free, 1)
                for own, other, h in ((low, high, 0), (high, low, 1)):
                    nc.vector.tensor_copy(k_st[0][other, par, h, cols], k_st[0][own, par, h, cols].bitcast(F32))
                dve.wait_ge(proj_free, 6 * jn + (gi + 1 + 2))
                for own, other, h in ((low, high, 0), (high, low, 1)):
                    last = nc.vector.tensor_copy(k_st[1][other, par, h, cols],
                                                 k_st[1][own, par, h, cols].bitcast(F32))
                last.then_inc(k_ready, 1)

            def turned_tile(par, j, n, kind, index):
                src = tile_ps[n % 2]
                dve.wait_ge(turned_hi, N_TILES * j + (PRE_TILES + n + 1))
                if kind == "V":
                    dst = v_cat[:, par, 4 * index:4 * index + 4, :, :, :]
                    nc.vector.tensor_tensor(dst[:, :, :, 1, :], src[:, :].rearrange("p (g h d) -> p g h d", g=4, h=2),
                                            dst[:, :, :, 0, :].bitcast(F32), ALU.subtract).then_inc(turned_lo, 1)
                    return
                g = index % GROUPS
                for first, count in runs_of(g):
                    at = first - blocks_of(g)[0]
                    last = nc.vector.tensor_tensor(
                        pT_part(pT[1], g, first, count),
                        src[:, at * P:(at + count) * P].rearrange("p (b q) -> p b q", b=count),
                        pT_part(pT[0], g, first, count).bitcast(F32), ALU.subtract)
                last.then_inc(turned_lo, 1)

            def add_bias(j, u):
                h, g = u // GROUPS, u % GROUPS
                n = P * len(blocks_of(g))
                table = bias_inner[:, h, :]
                if g == 0:
                    dve.wait_ge(bias_ready, 2 * j + (h + 1 + 2))
                    table = bias_full[:, h, P:NB]
                elif g == GROUPS - 1:
                    table = bias_full[:, h, 0:2 * P]
                dve.wait_ge(score_full, UNITS * j + (u + 1))
                if u:
                    sum_reciprocal(j, u - 1)
                else:
                    dve.wait_ge(exp_done, UNITS * j + (u + 1))
                    nc.vector.memset(spare[:, :], 0.0)
                nc.vector.tensor_tensor_reduce(out=score[:, u % 2, 0:n], in0=score_ps[u % 2][:, 0:n], in1=table,
                                               scale=-1.0, scalar=3e38, op0=ALU.add, op1=ALU.min,
                                               accum_out=nmax[:, u % 4:u % 4 + 1]).then_inc(score_done, 1)

            def sum_reciprocal(j, u):
                dve.wait_ge(exp_done, UNITS * j + (u + 1 + 2))
                nc.vector.reciprocal(recip[:, u % 4:u % 4 + 1], total[:, u % 4:u % 4 + 1]).then_inc(recip_done, 1)

            def normalise(j, u):
                n = P * len(blocks_of(u % GROUPS))
                dve.wait_ge(recip_done, UNITS * j + (u + 1))
                nc.vector.tensor_scalar(prob[:, u % 4, 0:n], prob[:, u % 4, 0:n], recip[:, u % 4:u % 4 + 1], None,
                                        ALU.mult).then_inc(prob_ready, 1)

            def out_sum(j, h, b):
                if h == 0 and b == 0:
                    dve.wait_ge(out_stored, 16 * j + 16)
                dve.wait_ge(low_done, 4 * j + (2 * h + b + 1))
                nc.vector.tensor_tensor(o_st[HEAD * h:HEAD * (h + 1), b * HALF:(b + 1) * HALF],
                                        out_ps[b][0:HEAD, :], o_low[0:HEAD, b, :], ALU.add).then_inc(out_done, 1)

            for credit, n in ((proj_free, 2), (score_done, 2), (turned_lo, 2), (out_done, 2)):
                dve.sem_inc(credit, n)
            for gi in (0, 1):
                evac(0, 0, gi)
            for t in range(2):
                turned_tile(0, -1, N_TILES - PRE_TILES + t, "V", t)
            for gi in range(2, 6):
                evac(0, 0, gi)

            def body(j, par, more, loads):
                for s in range(STEPS + 1):
                    if more and s in EVAC_STEP:
                        evac(1 - par, j + 1, EVAC_STEP.index(s))
                    if s < UNITS:
                        add_bias(j, s)
                    if s == UNITS:
                        sum_reciprocal(j, s - 1)
                    if 1 <= s <= UNITS:
                        normalise(j, s - 1)
                    for n, kind, index in tiles_at(s - 1, more):
                        turned_tile(1 - par, j, n, kind, index)
                    for h, b in out_evac_at(s):
                        out_sum(j, h, b)

            pairs_loop(dve, body)

        @block.tensor
        def _(pe):
            def project(par, jn, first, last):
                for m in range(first, last):
                    gi, i = divmod(m, GROUP_MMS)
                    kind, t = gi // 2, gi % 2
                    k, (wp, ap) = i // len(PASSES), PASSES[i % len(PASSES)]
                    if i == 0:
                        if t == 0:
                            pe.wait_ge(w_lo, 3 * jn + (kind + 1))
                        pe.wait_ge(proj_free, 6 * jn + (gi + 1))
                    mm = nc.tensor.matmul(proj_ps[gi % 2][:, :], w[wp][:, (par + kind) % 2, k, :],
                                          S.act[ap][:, k, t * HALF:(t + 1) * HALF],
                                          start=(i == 0), stop=(i == GROUP_MMS - 1))
                    if i == GROUP_MMS - 1:
                        mm.then_inc(proj_full, 1)

            def turn_v(j, n, t):
                pe.wait_ge(proj_free, 6 * j + (6 + t + 1 + 2))
                pe.wait_ge(turned_lo, N_TILES * j + (PRE_TILES + n + 1))
                for i in range(4):
                    mm = nc.tensor.transpose(tile_ps[n % 2][:, i * P:(i + 1) * P],
                                             v_T[:, t * HALF + i * P:t * HALF + (i + 1) * P], S.ident[:, :])
                mm.then_inc(turned, 1)

            def turn_p(j, n, u):
                pe.wait_ge(prob_ready, UNITS * j + (u + 1))
                pe.wait_ge(turned_lo, N_TILES * j + (PRE_TILES + n + 1))
                for i in range(len(blocks_of(u % GROUPS))):
                    mm = nc.tensor.transpose(tile_ps[n % 2][:, i * P:(i + 1) * P],
                                             prob[:, u % 4, i * P:(i + 1) * P], S.ident[:, :])
                mm.then_inc(turned, 1)

            def scores(par, j, u):
                h, g = u // GROUPS, u % GROUPS
                keys = blocks_of(g)
                cols = slice((g + keys[0]) * P, (g + keys[-1] + 1) * P)
                if u == 0:
                    pe.wait_ge(proj_free, 6 * j + (6 + 2))
                    pe.wait_ge(k_ready, 2 * j + 2)
                pe.wait_ge(score_done, UNITS * j + (u + 1))
                for part in range(2):
                    mm = nc.tensor.matmul(score_ps[u % 2][:, 0:P * len(keys)], q_st[:, par, h, g * P:(g + 1) * P],
                                          k_st[part][:, par, h, cols], start=(part == 0), stop=(part == 1))
                mm.then_inc(score_full, 1)

            def weigh_v(par, j, h, k, more):
                u = GROUPS * h + min(k + 1, GROUPS - 1)
                n = tiles_at(u + 2, more)[0][0]
                pe.wait_ge(turned_lo, N_TILES * j + (PRE_TILES + n + 1 + 2))
                if k == 0:
                    pe.wait_ge(out_done, 4 * j + (2 * h + 1))
                if k == 3:
                    pe.wait_ge(out_done, 4 * j + (2 * h + 2))
                queries = [q for q in (k - 1, k, k + 1) if 0 <= q < GROUPS]
                for b in range(2):
                    mine = [q for q in queries if q // 4 == b]
                    if not mine:
                        continue
                    for part in range(2):
                        at = mine[0] - (k - 1)
                        mm = nc.tensor.matmul(
                            out_ps[b][:, (mine[0] - 4 * b) * P:(mine[-1] + 1 - 4 * b) * P],
                            v_cat[:, par, k, h, :, :].rearrange("p a d -> p (a d)"),
                            pT[part][:, k % 4, at * P:(at + len(mine)) * P],
                            start=(part == 0 and k == (0 if b == 0 else 3)),
                            stop=(part == 1 and k == (4 if b == 0 else 7)), skip_group_check=True)
                mm.then_inc(pv_done, 1)

            pe.sem_inc(pv_done, 3)
            project(0, 0, 0, 2 * GROUP_MMS)
            for t in range(2):
                turn_v(-1, N_TILES - PRE_TILES + t, t)
            project(0, 0, 2 * GROUP_MMS, FILL)

            def body(j, par, more, loads):
                for s in range(STEPS):
                    if more and s < FILL_STEPS:
                        project(1 - par, j + 1, FILL * s // FILL_STEPS, FILL * (s + 1) // FILL_STEPS)
                    if s < UNITS:
                        scores(par, j, s)
                    for n, kind, index in tiles_at(s, more):
                        (turn_p if kind == "P" else turn_v)(j, n, index)
                    for h, k in pv_units_at(s):
                        weigh_v(par, j, h, k, more)

            pairs_loop(pe, body)


def load_rows(sp, S, slot, a, row, rows=1, cols=D, column=0):
    width = a.shape[-1]
    src = bass.AP(a.tensor, a.offset + row * width + column, [[width, P], [P * width, rows], [1, cols]])
    return sp.dma_start(S.raw[:, slot, :].rearrange("p (k n) -> p k n", k=rows), src)


def broadcast_row(a):
    return bass.AP(a.tensor, a.offset, [[0, P], [1, D]])


LN_STEPS = 6


def layer_norm_start(nc, dve, row, stats, mv, chain, at):
    for h in range(2):
        nc.vector.bn_stats(stats[:, h, :], row[:, h * HALF:(h + 1) * HALF]).then_inc(chain, 1)
    dve.wait_ge(chain, at + 2)
    nc.vector.memset(mv[:, 5:6], 0.0)
    nc.vector.bn_aggr(mv[:, 0:2], stats[:, :, :]).then_inc(chain, 1)
    dve.wait_ge(chain, at + 3)
    nc.vector.tensor_scalar_add(mv[:, 2:3], mv[:, 1:2], EPS).then_inc(chain, 1)


def layer_norm_finish(nc, dve, row, mv, gain, chain, at):
    nc.vector.reciprocal(mv[:, 4:5], mv[:, 3:4]).then_inc(chain, 1)
    dve.wait_ge(chain, at + 5)
    nc.vector.tensor_scalar(row, row, mv[:, 0:1], mv[:, 4:5], ALU.subtract, ALU.mult).then_inc(chain, 1)
    dve.wait_ge(chain, at + 6)
    return nc.vector.tensor_tensor(row, row, gain, ALU.mult)


def output_projection(nc, S, x, w_o, ln_g, ln_b, p, w_proj):
    with ExitStack() as ctx:
        def sb(name, shape, dt=F32):
            return ctx.enter_context(nc.sbuf_tensor(name, shape, dt))

        def sem(name):
            return ctx.enter_context(nc.semaphore(name))

        wo = [sb(f"w_o_{n}", [P, KC, D], F32R) for n in ("hi", "lo")]
        o_raw = sb("attention_tile", [P, 2, KC, P])
        o_part = [sb(f"attention_tile_{n}", [P, 2, KC, P], F32R) for n in ("hi", "lo")]
        xin = sb("x_tile", [P, 2, D])
        x1 = sb("x1_tile", [P, 2, D])
        gain, shift = sb("ln1_gain", [P, D]), sb("ln1_shift", [P, D])
        stats, mv = sb("ln1_stats", [P, 2, 2, 6]), sb("ln1_mean_var", [P, 2, 8])

        ln_in = sem("ln1_in")
        o_in = [sem(f"attention_tile_in{i}") for i in range(2)]
        x_in = [sem(f"x_tile_in{i}") for i in range(2)]
        wo_hi = sem("w_o_hi_done")
        wo_lo = sem("w_o_lo_done")
        o_hi = sem("attention_hi_done")
        o_lo = sem("attention_lo_done")
        y_full = sem("y_full")
        y_free = sem("y_free")
        chain = sem("ln1_chain")
        deviation = sem("ln1_deviation")
        scaled = sem("ln1_scaled")
        x1_ready = sem("x1_ready")
        x1_stored = [sem(f"x1_stored{i}") for i in range(2)]
        turned = sem("x1_turned")
        turned_hi = sem("x1_T_hi_done")
        turned_lo = sem("x1_T_lo_done")
        block = ctx.enter_context(nc.Block())

        def x1_T_tile(par, q):
            return S.ps[4 + 2 * par + q][:, :].rearrange("p (i t) -> p i t", i=4)

        def tiles_loop(eng, body):
            body(0, 0, 0)
            with eng.Fori(0, GROUPS // 2 - 1) as it:
                body(2 * it + 1, 1, it)
                body(2 * it + 2, 0, it + 1)
            body(GROUPS - 1, 1, GROUPS // 2 - 1)

        @block.sync
        def _(sp):
            def value(v):
                return in_register(sp, v)

            def load(t, par):
                place, split, read = value(t * P), value(t + 1), value(2 * t + 2)
                place_x = value(t * (GC * D))
                sp.wait_ge(o_lo, split)
                sp.dma_start(o_raw[:, par, :, :], bass.AP(S.oT.tensor, place, [[T, P], [P * T, KC], [1, P]]))\
                  .then_inc(o_in[par], 16)
                sp.wait_ge(y_free, read)
                sp.dma_start(xin[:, par, :], bass.AP(x.tensor, place_x, [[GRID_W * D, ROWS], [D, GC], [1, D]]))\
                  .then_inc(x_in[par], 16)

            for i in range(2):
                sp.sem_inc(x1_stored[i], 16)
            load(0, 0)
            for n in range(4, KC):
                sp.wait_ge(wo_lo, n - 3)
                load_rows(sp, S, n % 4, w_o, n * P).then_inc(S.wo_in[n % 4], 16)
            sp.dma_start(gain[:, :], broadcast_row(ln_g)).then_inc(ln_in, 16)
            sp.dma_start(shift[:, :], broadcast_row(ln_b)).then_inc(ln_in, 16)

            def body(t, par, nth):
                if not (isinstance(t, int) and t == GROUPS - 1):
                    load(t + 1, 1 - par)
                place, ready = value(t * (P * D)), value(t + 1)
                sp.wait_ge(x1_ready, ready)
                sp.dma_start(bass.AP(S.x1.tensor, place, [[D, P], [1, D]]), x1[:, par, :]).then_inc(x1_stored[par], 16)

            tiles_loop(sp, body)
            sp.wait_ge(wo_lo, KC)
            load_first_mlp_chunks(sp, S, p, w_proj)
            for i in range(2):
                sp.wait_ge(x1_stored[i], 16 * (GROUPS // 2 + 1))

        @block.gpsimd
        def _(pool):
            pool.sem_inc(o_lo, 2)

            def split(t, par):
                pool.wait_ge(o_hi, t + 1)
                nc.gpsimd.tensor_tensor(o_part[1][:, par, :, :], o_raw[:, par, :, :],
                                        o_part[0][:, par, :, :].bitcast(F32), ALU.subtract).then_inc(o_lo, 1)

            split(0, 0)
            pool.wait_ge(ln_in, 32)

            def body(t, par, nth):
                if not (isinstance(t, int) and t == GROUPS - 1):
                    split(t + 1, 1 - par)
                pool.wait_ge(scaled, t + 1)
                nc.gpsimd.tensor_tensor(x1[:, par, :], x1[:, par, :], shift[:, :], ALU.add).then_inc(x1_ready, 1)

            tiles_loop(pool, body)

        @block.scalar
        def _(act):
            def split(t, par, nth):
                act.wait_ge(o_in[par], 16 * nth + 16)
                act.wait_ge(y_full, 2 * t + 2)
                nc.scalar.activation(o_part[0][:, par, :, :], o_raw[:, par, :, :], ACT.Copy).then_inc(o_hi, 1)

            def turned_tile(t, par):
                for q in range(2):
                    act.wait_ge(turned, 2 * t + (q + 1))
                    nc.scalar.activation(S.act[0][:, 4 * q:4 * q + 4, bass.ds(t * P, P)], x1_T_tile(par, q),
                                         ACT.Copy).then_inc(turned_hi, 1)

            split(0, 0, 0)
            for n in range(KC):
                act.wait_ge(S.wo_in[n % 4], 16 * (n // 4 + 1))
                nc.scalar.activation(wo[0][:, n, :], S.raw[:, n % 4, :], ACT.Copy).then_inc(wo_hi, 1)

            def body(t, par, nth):
                if not (isinstance(t, int) and t == GROUPS - 1):
                    split(t + 1, 1 - par, nth + par)
                act.wait_ge(chain, LN_STEPS * t + 4)
                nc.scalar.activation(mv[:, par, 3:4], mv[:, par, 2:3], ACT.Sqrt).then_inc(deviation, 1)
                if not (isinstance(t, int) and t == 0):
                    turned_tile(t - 1, 1 - par)
                if isinstance(t, int) and t == GROUPS - 1:
                    turned_tile(t, par)

            tiles_loop(act, body)

        @block.vector
        def _(dve):
            for credit, n in ((y_free, 4), (turned_lo, 4)):
                dve.sem_inc(credit, n)
            for n in range(KC):
                dve.wait_ge(wo_hi, n + 1)
                nc.vector.tensor_tensor(wo[1][:, n, :], S.raw[:, n % 4, :], wo[0][:, n, :].bitcast(F32),
                                        ALU.subtract).then_inc(wo_lo, 1)
            dve.wait_ge(ln_in, 32)

            def body(t, par, nth):
                row = x1[:, par, :]
                dve.wait_ge(x_in[par], 16 * nth + 16)
                dve.wait_ge(x1_stored[par], 16 * nth + 16)
                for h in range(2):
                    cols = slice(h * HALF, (h + 1) * HALF)
                    dve.wait_ge(y_full, 2 * t + (h + 1 + 4))
                    nc.vector.scalar_tensor_tensor(out=row[:, cols], in0=xin[:, par, cols], scalar=ALPHA,
                                                   in1=S.ps[2 * par + h][:, :], op0=ALU.mult, op1=ALU.add)\
                        .then_inc(y_free, 1)
                dve.wait_ge(y_free, 2 * t + (2 + 4))
                layer_norm_start(nc, dve, row, stats[:, par], mv[:, par], chain, LN_STEPS * t)
                dve.wait_ge(deviation, t + 1)
                layer_norm_finish(nc, dve, row, mv[:, par], gain[:, :], chain, LN_STEPS * t).then_inc(scaled, 1)
                if not (isinstance(t, int) and t == 0):
                    turned_tile(t - 1, 1 - par)
                if isinstance(t, int) and t == GROUPS - 1:
                    turned_tile(t, par)

            def turned_tile(t, par):
                for q in range(2):
                    dve.wait_ge(turned_hi, 2 * t + (q + 1))
                    nc.vector.tensor_tensor(S.act[1][:, 4 * q:4 * q + 4, bass.ds(t * P, P)], x1_T_tile(par, q),
                                            S.act[0][:, 4 * q:4 * q + 4, bass.ds(t * P, P)].bitcast(F32),
                                            ALU.subtract).then_inc(turned_lo, 1)

            tiles_loop(dve, body)

        @block.tensor
        def _(pe):
            pe.sem_inc(y_full, 4)

            def turn(t, par):
                pe.wait_ge(x1_ready, t + 1)
                for q in range(2):
                    pe.wait_ge(turned_lo, 2 * t + (q + 1))
                    for i in range(4):
                        k = 4 * q + i
                        mm = nc.tensor.transpose(S.ps[4 + 2 * par + q][:, i * P:(i + 1) * P],
                                                 x1[:, par, k * P:(k + 1) * P], S.ident[:, :])
                    mm.then_inc(turned, 1)

            def body(t, par, nth):
                first = isinstance(t, int) and t == 0
                pe.wait_ge(o_lo, t + (1 + 2))
                for h in range(2):
                    pe.wait_ge(y_free, 2 * t + (h + 1))
                for k in range(KC):
                    if first:
                        pe.wait_ge(wo_lo, k + 1)
                    for h in range(2):
                        for n, (wp, ap) in enumerate(PASSES):
                            mm = nc.tensor.matmul(S.ps[2 * par + h][:, :], o_part[ap][:, par, k, :],
                                                  wo[wp][:, k, h * HALF:(h + 1) * HALF],
                                                  start=(k == 0 and n == 0), stop=(k == KC - 1 and n == 2))
                        if k == KC - 1:
                            mm.then_inc(y_full, 1)
                if not first:
                    turn(t - 1, 1 - par)
                if isinstance(t, int) and t == GROUPS - 1:
                    turn(t, par)

            tiles_loop(pe, body)


BLOCK_CHUNKS = 4
BLOCKS = FF // (BLOCK_CHUNKS * P)
PC = PLE // P


def load_first_mlp_chunks(sp, S, p, w_proj):
    for n in range(PC):
        load_rows(sp, S, n, w_proj, n * P).then_inc(S.ff_in[n], 16)
    for n in range(2):
        for i in range(4):
            sp.dma_start(S.raw[:, 2 + n, i * PLE:(i + 1) * PLE], token_tile(p, 4 * n + i)).then_inc(S.ff_in[2 + n], 16)


def mlp(nc, S, p, w_ff1, w_ff2, ln_g, ln_b, w_gate, w_proj, out):
    with ExitStack() as ctx:
        def sb(name, shape, dt=F32):
            return ctx.enter_context(nc.sbuf_tensor(name, shape, dt))

        def sem(name):
            return ctx.enter_context(nc.semaphore(name))

        y = sb("y", [P, GROUPS, D])
        hid = [sb(f"hidden_T_{n}", [P, BLOCK_CHUNKS, T], F32R) for n in ("hi", "lo")]
        wb = [sb(f"w_ff2_{n}", [P, BLOCK_CHUNKS, D], F32R) for n in ("hi", "lo")]
        w1 = [sb(f"w_ff1_{n}", [P, 2, KC, P], F32R) for n in ("hi", "lo")]
        gated = sb("gated", [P, 2, HALF])
        relu = sb("relu", [P, 2, HALF])
        stats, mv = sb("ln2_stats", [P, 2, 2, 6]), sb("ln2_mean_var", [P, 2, 8])

        y_in = [sem(f"y_in{t}") for t in range(GROUPS)]
        w_hi = sem("mlp_w_hi_done")
        w_lo = sem("mlp_w_lo_done")
        p_turned = sem("p_turned")
        p_hi = sem("p_hi_done")
        p_lo = sem("p_lo_done")
        gate_full = sem("gate_full")
        ple_full = sem("ple_full")
        wg_used = sem("w_gate_chunk_used")
        sigmoid = sem("sigmoid_done")
        product = sem("product_done")
        gate_done = sem("gate_done")
        ff1_full = sem("ff1_full")
        relu_done = sem("relu_done")
        square = sem("square_done")
        hid_hi = sem("hidden_hi_done")
        hid_lo = sem("hidden_lo_done")
        ff2_full = sem("ff2_full")
        y_added = sem("y_added")
        ln_in = sem("ln2_in")
        chain = sem("ln2_chain")
        deviation = sem("ln2_deviation")
        scaled = sem("ln2_scaled")
        out_ready = sem("out_ready")
        out_stored = sem("out_stored_final")
        block = ctx.enter_context(nc.Block())

        W_BLOCK = 2 + 8
        GROUPS1 = 2 * BLOCK_CHUNKS
        TILES2 = 2 * GROUPS

        def blocks_loop(eng, body):
            with eng.Fori(0, BLOCKS - 1) as b:
                body(b, False)
            body(BLOCKS - 1, True)

        @block.sync
        def _(sp):
            def value(v):
                return in_register(sp, v)

            def load_gate(half, i):
                load_rows(sp, S, i, w_gate, 2 * i * P, 2, HALF, half * HALF).then_inc(S.ff_in[i], 16)

            def load_ff1(c, column):
                src = bass.AP(w_ff1.tensor, column, [[FF, P], [P * FF, KC], [1, P]])
                sp.dma_start(S.raw[:, c, :].rearrange("p (k n) -> p k n", k=KC), src).then_inc(S.ff_in[c], 16)

            for i in range(BLOCK_CHUNKS):
                if i < 2:
                    sp.wait_ge(w_lo, i + 1)
                else:
                    sp.wait_ge(p_turned, 2 * (i - 1))
                load_gate(0, i)
            for t in range(GROUPS):
                sp.dma_start(y[:, t, :], S.x1[t]).then_inc(y_in[t], 16)
            for i in range(BLOCK_CHUNKS):
                sp.wait_ge(w_lo, 2 + i + 1)
                load_gate(1, i)
            for c in range(BLOCK_CHUNKS):
                sp.wait_ge(w_lo, 2 + 4 + c + 1)
                load_ff1(c, c * P)

            def body(b, last):
                row = value(b * (BLOCK_CHUNKS * P * D))
                for c in range(BLOCK_CHUNKS):
                    place = value(row + c * P * D)
                    split = value(8 * b + (c + 4 + 7))
                    sp.wait_ge(w_lo, split)
                    sp.dma_start(S.raw[:, c, :], bass.AP(w_ff2.tensor, place, [[D, P], [1, D]]))\
                      .then_inc(S.ff_in[c], 16)
                if last:
                    for c, a in ((0, ln_g), (1, ln_b)):
                        sp.wait_ge(w_lo, 8 * BLOCKS + c + 7)
                        sp.dma_start(S.raw[:, c, :], broadcast_row(a)).then_inc(ln_in, 16)
                    return
                for c in range(BLOCK_CHUNKS):
                    place = value(b * (BLOCK_CHUNKS * P) + (BLOCK_CHUNKS + c) * P)
                    split = value(8 * b + (8 + c + 7))
                    sp.wait_ge(w_lo, split)
                    load_ff1(c, place)

            blocks_loop(sp, body)
            for t in range(GROUPS):
                sp.wait_ge(out_ready, t + 1)
                sp.dma_start(token_tile(out, t), y[:, t, :]).then_inc(out_stored, 16)
            sp.wait_ge(out_stored, 16 * GROUPS)

        def target(part, m):
            if m < PC:
                return hid[part][:, PC + m, :]
            return wb[part][:, (m - PC) % 4, :]

        IN_BLOCK = [("ff1", 2), ("ff1", 3), ("ff2", 0), ("ff2", 1), ("ff2", 2), ("ff2", 3), ("ff1", 4), ("ff1", 5)]
        SPLIT_AFTER = [2, 4, 4, 5, 5, 6, 8, 8]

        def block_target(part, i):
            kind, c = IN_BLOCK[i]
            return (w1[part][:, c % 2, :, :].rearrange("p k n -> p (k n)") if kind == "ff1" else wb[part][:, c, :])

        @block.gpsimd
        def _(pool):
            def low(dst, hi, slot, count):
                pool.wait_ge(w_hi, count)
                nc.gpsimd.tensor_tensor(dst, S.raw[:, slot, :], hi.bitcast(F32), ALU.subtract).then_inc(w_lo, 1)

            for m in range(PC + 8):
                low(target(1, m), target(0, m), m % 2 if m < PC else (m - PC) % 4, m + 1)
            for c in range(2):
                low(block_target(1, 6 + c), block_target(0, 6 + c), c, W_BLOCK + c + 1)

            def body(b, last):
                for i in range(GROUPS1 + 1):
                    for s, after in enumerate(SPLIT_AFTER):
                        if after == i and not (last and s >= 6):
                            low(block_target(1, s), block_target(0, s), IN_BLOCK[s][1] % 4, 8 * b + (W_BLOCK + 2 + s + 1))
                    if i < GROUPS1:
                        pool.wait_ge(relu_done, GROUPS1 * b + (i + 1))
                        nc.gpsimd.tensor_tensor(relu[:, i % 2, :], relu[:, i % 2, :], relu[:, i % 2, :], ALU.mult)\
                            .then_inc(square, 1)

            blocks_loop(pool, body)
            pool.wait_ge(ln_in, 32)
            for t in range(GROUPS):
                pool.wait_ge(scaled, t + 1)
                nc.gpsimd.tensor_tensor(y[:, t, :], y[:, t, :], S.raw[:, 1, :], ALU.add).then_inc(out_ready, 1)

        @block.scalar
        def _(act):
            def high(dst, slot, loads):
                act.wait_ge(S.ff_in[slot], loads)
                nc.scalar.activation(dst, S.raw[:, slot, :], ACT.Copy).then_inc(w_hi, 1)

            P_LOADS = (16, 16, 64, 64)
            for m in range(PC):
                high(target(0, m), m, 16)
            for n in range(4):
                act.wait_ge(p_turned, n + 1)
                nc.scalar.activation(hid[0][:, n % 2, (n // 2) * HALF:(n // 2 + 1) * HALF], S.ps[4 + n][:, :],
                                     ACT.Copy).then_inc(p_hi, 1)
            for i in range(4):
                high(target(0, PC + i), i, P_LOADS[i] + 16)

            def sigmoids(half):
                for t in range(GROUPS):
                    u = GROUPS * half + t
                    act.wait_ge(gate_full, u + 1)
                    act.wait_ge(gate_done, u + 1)
                    nc.scalar.activation(gated[:, u % 2, :], S.ps[u % 2][:, :], ACT.Sigmoid).then_inc(sigmoid, 1)

            sigmoids(0)
            for i in range(4):
                if i < 3:
                    act.wait_ge(wg_used, i + 1)
                high(target(0, PC + 4 + i), i, P_LOADS[i] + 32)
            for c in range(2):
                high(block_target(0, 6 + c), c, P_LOADS[c] + 48)
            sigmoids(1)

            def body(b, last):
                for i in range(GROUPS1 + 1):
                    for s, after in enumerate(SPLIT_AFTER):
                        if after == i and not (last and s >= 6):
                            kind, c = IN_BLOCK[s]
                            if kind == "ff1" and s >= 6:
                                act.wait_ge(ff1_full, GROUPS1 * b + (4 + 2 * (c - 2) + 2))
                            loads = {0: 4, 1: 5}[0 if kind == "ff1" else 1] + (2 if c >= 4 else 0)
                            slot = c % 4
                            high(block_target(0, s), slot, 32 * b + (P_LOADS[slot] + 16 * (loads - 1)))
                    if i < GROUPS1:
                        act.wait_ge(ff1_full, GROUPS1 * b + (i + 1 + 4))
                        act.wait_ge(hid_lo, GROUPS1 * b + (i + 1 + 2))
                        nc.scalar.activation(relu[:, i % 2, :], S.ps[i % 4][:, :], ACT.Relu).then_inc(relu_done, 1)
                        act.wait_ge(square, GROUPS1 * b + (i + 1))
                        nc.scalar.activation(hid[0][:, i // 2, (i % 2) * HALF:(i % 2 + 1) * HALF], relu[:, i % 2, :],
                                             ACT.Copy).then_inc(hid_hi, 1)

            blocks_loop(act, body)
            for t in range(GROUPS):
                act.wait_ge(chain, LN_STEPS * t + 4)
                nc.scalar.activation(mv[:, t % 2, 3:4], mv[:, t % 2, 2:3], ACT.Sqrt).then_inc(deviation, 1)

        @block.vector
        def _(dve):
            for credit, n in ((gate_done, 2), (hid_lo, 4), (y_added, 4)):
                dve.sem_inc(credit, n)
            for n in range(4):
                dve.wait_ge(p_hi, n + 1)
                cols = slice((n // 2) * HALF, (n // 2 + 1) * HALF)
                nc.vector.tensor_tensor(hid[1][:, n % 2, cols], S.ps[4 + n][:, :], hid[0][:, n % 2, cols].bitcast(F32),
                                        ALU.subtract).then_inc(p_lo, 1)
            for u in range(2 * GROUPS):
                half, t = divmod(u, GROUPS)
                cols = slice(half * HALF, (half + 1) * HALF)
                dve.wait_ge(sigmoid, u + 1)
                dve.wait_ge(ple_full, u + 1)
                nc.vector.tensor_tensor(gated[:, u % 2, :], gated[:, u % 2, :], S.ps[2 + u % 2][:, :], ALU.mult)\
                    .then_inc(product, 1)
                dve.wait_ge(y_in[t], 16)
                dve.wait_ge(product, u + 1)
                nc.vector.scalar_tensor_tensor(out=y[:, t, cols], in0=y[:, t, cols], scalar=ALPHA,
                                               in1=gated[:, u % 2, :], op0=ALU.mult, op1=ALU.add)\
                    .then_inc(gate_done, 1)

            def body(b, last):
                for i in range(GROUPS1):
                    dve.wait_ge(hid_hi, GROUPS1 * b + (i + 1))
                    cols = slice((i % 2) * HALF, (i % 2 + 1) * HALF)
                    nc.vector.tensor_tensor(hid[1][:, i // 2, cols], relu[:, i % 2, :],
                                            hid[0][:, i // 2, cols].bitcast(F32), ALU.subtract).then_inc(hid_lo, 1)
                for n in range(TILES2):
                    t, h = divmod(n, 2)
                    cols = slice(h * HALF, (h + 1) * HALF)
                    dve.wait_ge(ff2_full, TILES2 * b + (n + 1))
                    nc.vector.tensor_tensor(y[:, t, cols], y[:, t, cols], S.ps[4 + n % 4][:, :], ALU.add)\
                        .then_inc(y_added, 1)
                    if last and h == 1:
                        if t == 0:
                            dve.wait_ge(ln_in, 32)
                        dve.wait_ge(y_added, TILES2 * b + (n + 1 + 4))
                        layer_norm_start(nc, dve, y[:, t, :], stats[:, t % 2], mv[:, t % 2], chain, LN_STEPS * t)
                        dve.wait_ge(deviation, t + 1)
                        layer_norm_finish(nc, dve, y[:, t, :], mv[:, t % 2], S.raw[:, 0, :], chain, LN_STEPS * t)\
                            .then_inc(scaled, 1)

            blocks_loop(dve, body)

        @block.tensor
        def _(pe):
            pe.sem_inc(ff1_full, 4)
            for n in range(4):
                c, th = n % 2, n // 2
                pe.wait_ge(S.ff_in[2 + th], 64)
                for i in range(4):
                    mm = nc.tensor.transpose(S.ps[4 + n][:, i * P:(i + 1) * P],
                                             S.raw[:, 2 + th, i * PLE + c * P:i * PLE + (c + 1) * P], S.ident[:, :])
                mm.then_inc(p_turned, 1)

            def gate_columns(part, k):
                return wb[part][:, k // 2, (k % 2) * HALF:(k % 2 + 1) * HALF]

            for u in range(2 * GROUPS):
                half, t = divmod(u, GROUPS)
                tokens = slice(t * P, (t + 1) * P)
                pe.wait_ge(gate_done, u + 1)
                for k in range(KC):
                    if t == 0 and k % 2 == 0:
                        pe.wait_ge(w_lo, PC + 4 * half + k // 2 + 1)
                    for n, (wp, ap) in enumerate(PASSES):
                        mm = nc.tensor.matmul(S.ps[u % 2][:, :], S.act[ap][:, k, tokens], gate_columns(wp, k),
                                              start=(k == 0 and n == 0), stop=(k == KC - 1 and n == 2))
                    if u == GROUPS - 1 and k % 2 and k < KC - 1:
                        mm.then_inc(wg_used, 1)
                mm.then_inc(gate_full, 1)
                if u == 0:
                    pe.wait_ge(p_lo, 4)
                for k in range(PC):
                    for n, (wp, ap) in enumerate(PASSES):
                        mm = nc.tensor.matmul(S.ps[2 + u % 2][:, :], hid[ap][:, k, tokens],
                                              hid[wp][:, PC + k, half * HALF:(half + 1) * HALF],
                                              start=(k == 0 and n == 0), stop=(k == PC - 1 and n == 2))
                mm.then_inc(ple_full, 1)

            pe.wait_ge(gate_done, 2 * GROUPS + 2)

            def body(b, last):
                for i in range(GROUPS1):
                    c, th = divmod(i, 2)
                    if th == 0:
                        pe.wait_ge(w_lo, 8 * b + (W_BLOCK + c + 1))
                    pe.wait_ge(hid_lo, GROUPS1 * b + (i + 1))
                    for k in range(KC):
                        for n, (wp, ap) in enumerate(PASSES):
                            mm = nc.tensor.matmul(S.ps[i % 4][:, :], w1[wp][:, c % 2, k, :],
                                                  S.act[ap][:, k, th * HALF:(th + 1) * HALF],
                                                  start=(k == 0 and n == 0), stop=(k == KC - 1 and n == 2))
                    mm.then_inc(ff1_full, 1)
                for n in range(TILES2):
                    t, h = divmod(n, 2)
                    if n == 0:
                        pe.wait_ge(w_lo, 8 * b + (W_BLOCK + 8))
                    if n in (0, TILES2 // 2):
                        pe.wait_ge(hid_lo, GROUPS1 * b + (GROUPS1 - 1 + (n > 0) + 4))
                    pe.wait_ge(y_added, TILES2 * b + (n + 1))
                    for k in range(BLOCK_CHUNKS):
                        for i, (wp, ap) in enumerate(PASSES):
                            mm = nc.tensor.matmul(S.ps[4 + n % 4][:, :], hid[ap][:, k, t * P:(t + 1) * P],
                                                  wb[wp][:, k, h * HALF:(h + 1) * HALF],
                                                  start=(k == 0 and i == 0), stop=(k == BLOCK_CHUNKS - 1 and i == 2))
                    mm.then_inc(ff2_full, 1)

            blocks_loop(pe, body)


INPUTS = ["x", "p", "na_w_qkv", "na_rpb", "na_w_o", "ln1_g", "ln1_b", "w_ff1", "w_ff2", "ln2_g", "ln2_b",
          "w_ple_gate", "w_ple_proj"]


def column_mask():
    query = np.arange(P) % GC
    key = np.arange(3 * GC).reshape(3, 1, GC)
    inside = (key[None] >= query[:, None, None, None]) & (key[None] < query[:, None, None, None] + KW)
    return np.broadcast_to(np.where(inside, 0.0, MASKED), (P, 3, ROWS, GC)).reshape(P, NB).astype(np.float32)


def kernel(**inputs):
    import concourse.bacc as bacc
    from concourse.bass_utils import run_bass_kernel_spmd

    nc = bacc.Bacc("TRN2", target_bir_lowering=False, num_devices=1)
    arrays = {f"in_{name}": np.ascontiguousarray(inputs[name]) for name in INPUTS}
    arrays["column_mask_table"] = column_mask()
    args = [nc.dram_tensor(name, a.shape, mybir.dt.from_np(a.dtype), kind="ExternalInput").ap()
            for name, a in arrays.items()]
    shape = inputs["x"].shape
    args.append(nc.dram_tensor("out", shape, F32, kind="ExternalOutput").ap())
    build_program(nc, *args)
    result = run_bass_kernel_spmd(nc, [arrays], core_ids=[0])
    return result.results[0]["out"]
```

```python
from contextlib import ExitStack

import numpy as np

import concourse.bass as bass
from concourse import mybir

P = 128
D = 1024
T = 1024
HEAD = 64
HEADS = D // HEAD
PAIRS = HEADS // 2
GRID_W = 64
ROWS = T // GRID_W
KH, KW = 8, 16
GC = 8
GROUPS = T // P
KC = D // P
HALF = 512
DR, DC = 2 * KH - 1, 2 * KW - 1
NB = 3 * P
FF = 4 * D
PLE = 256
ALPHA = float(2 ** 0.25)
EPS = 1e-6
MASKED = -1e38

F32 = mybir.dt.float32
F32R = mybir.dt.float32r
ALU = mybir.AluOpType
ACT = mybir.ActivationFunctionType

V_, K_, Q_ = range(3)
W_COLUMN = {V_: 2 * D, K_: D, Q_: 0}
PASSES = ((0, 0), (0, 1), (1, 0))

UNITS = 2 * GROUPS
STEPS = UNITS + 4
GROUP_MMS = KC * len(PASSES)
FILL = 6 * GROUP_MMS
FILL_STEPS = STEPS - 1
EVAC_STEP = [(GROUP_MMS * (gi + 1) - 1) * FILL_STEPS // FILL + 1 for gi in range(6)]
V_TURN_STEP = (4, 7)


def blocks_of(g):
    return [d for d in (-1, 0, 1) if 0 <= g + d < GROUPS]


def runs_of(g):
    out = []
    for d in blocks_of(g):
        if out and (g + d) % 4:
            out[-1][1] += 1
        else:
            out.append([d, 1])
    return out


def pv_units_at(s):
    out = []
    for h in range(2):
        for k in range(GROUPS):
            if s == GROUPS * h + min(k + 1, GROUPS - 1) + 4:
                out.append((h, k))
    return out


def out_evac_at(s):
    return [(h, b) for h in range(2) for b in range(2) if s == GROUPS * h + (10 if b == 0 else 12)]


class Shared:
    pass


def build_program(nc, x, p, w_qkv, rpb, w_o, ln1_g, ln1_b, w_ff1, w_ff2, ln2_g, ln2_b, w_gate, w_proj, mask, out):
    with ExitStack() as ctx:
        S = Shared()
        S.raw = ctx.enter_context(nc.sbuf_tensor("weight_raw", [P, 4, D], F32))
        S.ident = ctx.enter_context(nc.sbuf_tensor("identity", [P, P], F32))
        S.act = [ctx.enter_context(nc.sbuf_tensor(f"act_T_{n}", [P, KC, T], F32R)) for n in ("hi", "lo")]
        S.ps = [ctx.enter_context(nc.psum_tensor(f"bank{i}", [P, HALF], F32)) for i in range(8)]
        S.oT = nc.dram_tensor("attention_T", [PAIRS, P, T], F32).ap()
        S.rpb_rows = nc.dram_tensor("rpb_rows", [GC, HEADS, DR, 3 * GC], F32).ap()
        S.rpb_stored = ctx.enter_context(nc.semaphore("rpb_rows_stored"))
        S.raw_in, S.wo_in, S.ff_in = ([ctx.enter_context(nc.semaphore(f"{n}_raw_in{i}")) for i in range(4)]
                                      for n in ("qkv", "w_o", "mlp"))
        S.x1 = nc.dram_tensor("x_after_attention", [GROUPS, P, D], F32).ap()
        with ExitStack() as first:
            S.w = [first.enter_context(nc.sbuf_tensor(f"w_qkv_{n}", [P, 2, KC, P], F32R)) for n in ("hi", "lo")]
            S.w_hi, S.w_lo = (first.enter_context(nc.semaphore(f"w_{n}_done")) for n in ("hi", "lo"))
            transpose_input(nc, S, x, w_qkv, rpb)
            attention(nc, S, w_qkv, mask, w_o)
        output_projection(nc, S, x, w_o, ln1_g, ln1_b, w_gate)
        mlp(nc, S, p, w_ff1, w_ff2, ln2_g, ln2_b, w_gate, w_proj, out)


def in_register(engine, v):
    return v if isinstance(v, int) else engine.snap(v)


def qkv_chunk(w_qkv, kind, offset):
    return bass.AP(w_qkv.tensor, w_qkv.offset + W_COLUMN[kind] + offset, [[3 * D, P], [P * 3 * D, KC], [1, P]])


def transpose_input(nc, S, x, w_qkv, rpb):
    with ExitStack() as ctx:
        xin = ctx.enter_context(nc.sbuf_tensor("x_tokens", [P, GROUPS, D], F32))
        x_in = [ctx.enter_context(nc.semaphore(f"x_in{g}")) for g in range(GROUPS)]
        zeroed = ctx.enter_context(nc.semaphore("identity_zeroed"))
        ident_ready = ctx.enter_context(nc.semaphore("identity_ready"))
        turned = ctx.enter_context(nc.semaphore("x_turned"))
        hi_done = ctx.enter_context(nc.semaphore("x_hi_done"))
        lo_done = ctx.enter_context(nc.semaphore("x_lo_done"))
        tiles = [(g, q) for g in range(GROUPS) for q in range(2)]
        block = ctx.enter_context(nc.Block())

        @block.sync
        def _(sp):
            for g in range(GROUPS):
                sp.dma_start(xin[:, g, :], token_tile(x, g)).then_inc(x_in[g], 16)
                if g in (1, 3, 5):
                    kind = g // 2
                    sp.dma_start(S.raw[:, kind, :].rearrange("p (k n) -> p k n", k=KC),
                                 qkv_chunk(w_qkv, kind, 0)).then_inc(S.raw_in[kind], 16)
            for c in range(GC):
                src = bass.AP(rpb.tensor, rpb.offset + KW - 1 - GC - c, [[DC, HEADS * DR], [1, 3 * GC]])
                sp.dma_start(S.rpb_rows[c].rearrange("h r w -> (h r) w"), src).then_inc(S.rpb_stored, 16)

        @block.gpsimd
        def _(pool):
            nc.gpsimd.memset(S.ident[:, :], 0.0).then_inc(zeroed, 1)
            pool.wait_ge(zeroed, 1)
            nc.gpsimd.affine_select(out=S.ident[:, :], in_=S.ident[:, :], compare_op=ALU.not_equal, fill=1.0,
                                    base=0, pattern=[[-1, P]], channel_multiplier=1).then_inc(ident_ready, 1)

        @block.tensor
        def _(pe):
            pe.wait_ge(ident_ready, 1)
            for n, (g, q) in enumerate(tiles):
                pe.wait_ge(x_in[g], 16)
                if n >= 8:
                    pe.wait_ge(lo_done, n - 7)
                for i in range(4):
                    k = 4 * q + i
                    last = nc.tensor.transpose(S.ps[n % 8][:, i * P:(i + 1) * P], xin[:, g, k * P:(k + 1) * P],
                                               S.ident[:, :])
                last.then_inc(turned, 1)

        def dest(part, g, q):
            return S.act[part][:, 4 * q:4 * q + 4, g * P:(g + 1) * P]

        def tile(n):
            return S.ps[n % 8][:, :].rearrange("p (i t) -> p i t", i=4)

        @block.scalar
        def _(act):
            for n, (g, q) in enumerate(tiles):
                act.wait_ge(turned, n + 1)
                nc.scalar.activation(dest(0, g, q), tile(n), ACT.Copy).then_inc(hi_done, 1)
            for kind in (V_, K_):
                act.wait_ge(S.raw_in[kind], 16)
                nc.scalar.activation(S.w[0][:, kind, :, :], S.raw[:, kind, :].rearrange("p (k n) -> p k n", k=KC),
                                     ACT.Copy).then_inc(S.w_hi, 1)

        @block.vector
        def _(dve):
            for n, (g, q) in enumerate(tiles):
                dve.wait_ge(hi_done, n + 1)
                nc.vector.tensor_tensor(dest(1, g, q), tile(n), dest(0, g, q).bitcast(F32),
                                        ALU.subtract).then_inc(lo_done, 1)
            for kind in (V_, K_):
                dve.wait_ge(S.w_hi, kind + 1)
                nc.vector.tensor_tensor(S.w[1][:, kind, :, :], S.raw[:, kind, :].rearrange("p (k n) -> p k n", k=KC),
                                        S.w[0][:, kind, :, :].bitcast(F32), ALU.subtract).then_inc(S.w_lo, 1)


def token_tile(a, g):
    width = a.shape[-1]
    return bass.AP(a.tensor, a.offset + g * GC * width, [[GRID_W * width, ROWS], [width, GC], [1, width]])


def attention(nc, S, w_qkv, mask, w_o):
    with ExitStack() as ctx:
        def sb(name, shape, dt=F32):
            return ctx.enter_context(nc.sbuf_tensor(name, shape, dt))

        def sem(name):
            return ctx.enter_context(nc.semaphore(name))

        q_st = sb("q_hi_lo", [P, 2, 2, T], F32R)
        k_st = [sb(f"k_{n}_twice", [P, 2, 2, T], F32R) for n in ("hi", "lo")]
        v_T = sb("v_T", [P, T])
        v_cat = sb("v_hi_lo", [P, 2, GROUPS, 2, 2, HEAD], F32R)
        bias_in = sb("bias_in", [P, 2, ROWS, 3 * GC])
        bias_inner = sb("bias_inner", [P, 2, NB])
        bias_full = sb("bias_full", [P, 2, NB])
        col_mask = sb("column_mask", [P, NB])
        score = sb("negated_scores", [P, 2, NB])
        nmax = sb("negated_max", [P, 4])
        total = sb("exp_total", [P, 4])
        recip = sb("total_reciprocal", [P, 4])
        spare = sb("spare", [P, 1])
        prob = sb("probabilities", [P, 4, NB])
        pT = [sb(f"prob_T_{n}", [P, 4, NB], F32R) for n in ("hi", "lo")]
        o_low = sb("out_low_part", [P, 2, HALF])
        o_st = sb("out_T", [P, T])

        proj_full = sem("proj_full")
        proj_free = sem("proj_free")
        proj_hi = sem("proj_hi_done")
        bias_loaded = [sem(f"bias_loaded{h}") for h in range(2)]
        mask_loaded = sem("mask_loaded")
        bias_reset = sem("bias_reset")
        bias_ready = sem("bias_ready")
        score_full = sem("score_full")
        score_done = sem("score_done")
        exp_done = sem("exp_done")
        recip_done = sem("recip_done")
        prob_ready = sem("prob_ready")
        k_doubled = sem("k_doubled")
        v_turned = sem("v_turned")
        v_hi = sem("v_hi_done")
        v_lo = sem("v_lo_done")
        turned = sem("tile_turned")
        turned_hi = sem("tile_hi_done")
        turned_lo = sem("tile_lo_done")
        pv_done = sem("pv_done")
        low_done = sem("out_low_done")
        out_done = sem("out_done")
        out_stored = sem("out_stored")
        block = ctx.enter_context(nc.Block())

        w, w_hi, w_lo = S.w, S.w_hi, S.w_lo
        proj_ps, score_ps, tile_ps, out_ps = S.ps[0:2], S.ps[2:4], S.ps[4:6], S.ps[6:8]
        Q_SCALE = HEAD ** -0.5

        def pT_part(buf, g, first, count):
            slot = (g + first) % 4
            base = buf[:, slot, (1 - first) * P:(2 - first) * P]
            return bass.AP(base.tensor, base.offset, [list(base.ap[0]), [NB - P, count], [1, P]])

        def pairs_loop(eng, body):
            with eng.Fori(0, PAIRS // 2 - 1) as it:
                for par in range(2):
                    body(2 * it + par, par, True, True)
            body(PAIRS - 2, 0, True, False)
            body(PAIRS - 1, 1, False, False)

        @block.sync
        def _(sp):
            def value(v):
                return in_register(sp, v)

            def load_w(kind, offset):
                sp.dma_start(S.raw[:, kind, :].rearrange("p (k n) -> p k n", k=KC),
                             qkv_chunk(w_qkv, kind, offset)).then_inc(S.raw_in[kind], 16)

            def load_bias(h, offset, built):
                built = value(built)
                for qr in range(ROWS):
                    r0 = min(max(qr - KH // 2, 0), ROWS - KH)
                    start = value(offset + (r0 - qr + KH - 1) * 3 * GC)
                    if qr == 0:
                        sp.wait_ge(bias_ready, built)
                    src = bass.AP(S.rpb_rows.tensor, start, [[HEADS * DR * 3 * GC, GC], [1, KH * 3 * GC]])
                    sp.dma_start(bias_in[qr * GC:(qr + 1) * GC, h, r0:r0 + KH, :].rearrange("p r w -> p (r w)"), src)\
                      .then_inc(bias_loaded[h], 16)

            def k_twice(par, jn):
                written = value(6 * jn + (4 + 2))
                for h in range(2):
                    own, other = slice(HEAD * h, HEAD * (h + 1)), slice(HEAD * (1 - h), HEAD * (2 - h))
                    for part in range(2):
                        if h == 0 and part == 0:
                            sp.wait_ge(proj_free, written)
                        sp.dma_start(k_st[part][other, par, h, :].bitcast(F32),
                                     k_st[part][own, par, h, :].bitcast(F32)).then_inc(k_doubled, 16)

            sp.sem_inc(out_stored, 16)
            sp.dma_start(col_mask[:, :], mask).then_inc(mask_loaded, 16)
            sp.wait_ge(bias_reset, 1)
            sp.wait_ge(S.rpb_stored, 16 * GC)
            sp.sem_inc(bias_ready, 2)
            for h in range(2):
                load_bias(h, h * DR * 3 * GC, 2)
            for kind in range(3):
                sp.wait_ge(w_hi, kind + 1)
                sp.wait_ge(w_lo, kind + 1)
                load_w(kind, P)
            k_twice(0, 0)
            for h in range(2):
                load_bias(h, (2 + h) * DR * 3 * GC, h + 1 + 2)

            def body(j, par, more, loads):
                if loads:
                    column = value(j * P + 2 * P)
                    for kind in range(3):
                        split = value(3 * j + (3 + kind + 1))
                        sp.wait_ge(w_hi, split)
                        sp.wait_ge(w_lo, split)
                        load_w(kind, column)
                for h in range(2):
                    if loads:
                        load_bias(h, j * (2 * DR * 3 * GC) + (4 + h) * DR * 3 * GC, 2 * j + (2 + h + 1 + 2))
                    if more and h == 0:
                        k_twice(1 - par, j + 1)
                place, summed = value(j * (P * T)), value(4 * j + (4 + 2))
                sp.wait_ge(out_done, summed)
                sp.dma_start(bass.AP(S.oT.tensor, place, [[T, P], [1, T]]), o_st[:, :]).then_inc(out_stored, 16)

            pairs_loop(sp, body)
            sp.wait_ge(w_lo, 3 * PAIRS)
            for n in range(4):
                load_rows(sp, S, n, w_o, n * P).then_inc(S.wo_in[n], 16)
            sp.wait_ge(out_stored, 16 * (PAIRS + 1))

        @block.gpsimd
        def _(pool):
            nc.gpsimd.memset(bias_in[:, :, :, :], MASKED).then_inc(bias_reset, 1)
            pool.wait_ge(mask_loaded, 16)

            def split(slot, kind, count):
                pool.wait_ge(w_hi, count)
                nc.gpsimd.tensor_tensor(w[1][:, slot, :, :], S.raw[:, kind, :].rearrange("p (k n) -> p k n", k=KC),
                                        w[0][:, slot, :, :].bitcast(F32), ALU.subtract).then_inc(w_lo, 1)

            def build_bias(h, loads):
                pool.wait_ge(bias_loaded[h], loads)
                src = bias_in[:, h, :, :].rearrange("p r (d c) -> p d r c", d=3)
                shape = dict(d=3, r=ROWS)
                nc.gpsimd.tensor_tensor(bias_inner[:, h, :].rearrange("p (d r c) -> p d r c", **shape), src,
                                        col_mask[:, :].rearrange("p (d r c) -> p d r c", **shape), ALU.add)
                nc.gpsimd.tensor_copy(bias_full[:, h, :].rearrange("p (d r c) -> p d r c", **shape), src)\
                    .then_inc(bias_ready, 1)

            for h in range(2):
                build_bias(h, 16 * ROWS)
            split(0, Q_, 3)
            split(1, V_, 4)

            def body(j, par, more, loads):
                if more:
                    split((par + 1 + K_) % 2, K_, 3 * j + (3 + K_ + 1))
                    split((par + 1 + Q_) % 2, Q_, 3 * j + (3 + Q_ + 1))
                    pool.wait_ge(score_done, UNITS * j + (GROUPS + 2))
                    build_bias(0, 16 * ROWS * j + 2 * 16 * ROWS)
                if loads:
                    split(par % 2, V_, 3 * j + (6 + V_ + 1))
                if more:
                    pool.wait_ge(score_done, UNITS * j + (UNITS + 2))
                    build_bias(1, 16 * ROWS * j + 2 * 16 * ROWS)

            pairs_loop(pool, body)

        @block.scalar
        def _(act):
            def split(slot, kind, loads):
                act.wait_ge(S.raw_in[kind], loads)
                nc.scalar.activation(w[0][:, slot, :, :], S.raw[:, kind, :].rearrange("p (k n) -> p k n", k=KC),
                                     ACT.Copy).then_inc(w_hi, 1)

            def evac(par, jn, gi):
                kind, t = gi // 2, gi % 2
                if kind == V_:
                    return
                act.wait_ge(proj_full, 6 * jn + (gi + 1))
                dst = q_st if kind == Q_ else k_st[0]
                for h in range(2):
                    rows = slice(HEAD * h, HEAD * (h + 1))
                    nc.scalar.activation(dst[rows, par, h, t * HALF:(t + 1) * HALF], proj_ps[gi % 2][rows, :],
                                         ACT.Copy, scale=Q_SCALE if kind == Q_ else 1.0).then_inc(proj_hi, 1)

            def turned_v(par, jn, t):
                act.wait_ge(v_turned, 2 * jn + (t + 1))
                nc.scalar.activation(v_cat[:, par, 4 * t:4 * t + 4, :, 0, :],
                                     proj_ps[t][:, :].rearrange("p (g h d) -> p g h d", g=4, h=2),
                                     ACT.Copy).then_inc(v_hi, 1)

            def turned_tile(j, u):
                g = u % GROUPS
                act.wait_ge(turned, UNITS * j + (u + 1))
                act.wait_ge(pv_done, UNITS * j + (u + 1))
                for first, count in runs_of(g):
                    at = first - blocks_of(g)[0]
                    last = nc.scalar.activation(pT_part(pT[0], g, first, count),
                                                tile_ps[u % 2][:, at * P:(at + count) * P].rearrange(
                                                    "p (b q) -> p b q", b=count), ACT.Copy)
                last.then_inc(turned_hi, 1)

            def softmax_exp(j, u):
                g = u % GROUPS
                n = P * len(blocks_of(g))
                act.wait_ge(score_done, UNITS * j + (u + 1 + 2))
                nc.scalar.activation(prob[:, u % 4, 0:n], score[:, u % 2, 0:n], ACT.Exp, scale=-1.0,
                                     bias=nmax[:, u % 4:u % 4 + 1],
                                     accum_out=total[:, u % 4:u % 4 + 1]).then_inc(exp_done, 1)

            def out_low(j, h, b):
                act.wait_ge(pv_done, UNITS * j + (GROUPS * h + (5 if b == 0 else 8) + 3))
                act.wait_ge(out_done, 4 * j + (2 * h + b + 1))
                nc.scalar.activation(o_low[0:HEAD, b, :], out_ps[b][HEAD:P, :], ACT.Copy).then_inc(low_done, 1)

            act.sem_inc(exp_done, 2)
            act.wait_ge(proj_full, 2)
            split(0, Q_, 16)
            for t in range(2):
                turned_v(0, 0, t)
            for gi in (2, 3):
                evac(0, 0, gi)
            split(1, V_, 32)
            for gi in (4, 5):
                evac(0, 0, gi)

            def body(j, par, more, loads):
                for s in range(STEPS + 1):
                    if 3 <= s < UNITS + 3:
                        turned_tile(j, s - 3)
                    for h, b in out_evac_at(s):
                        out_low(j, h, b)
                    if more and s in EVAC_STEP[2:]:
                        evac(1 - par, j + 1, EVAC_STEP.index(s))
                    if more and s - 1 in V_TURN_STEP:
                        turned_v(1 - par, j + 1, V_TURN_STEP.index(s - 1))
                    if s < UNITS:
                        softmax_exp(j, s)
                    if not more:
                        continue
                    if s == 1:
                        split((par + 1 + K_) % 2, K_, 16 * j + 32)
                    if s == EVAC_STEP[1] + 2:
                        act.wait_ge(proj_full, 6 * j + (6 + 2))
                        split((par + 1 + Q_) % 2, Q_, 16 * j + 32)
                    if loads and s == EVAC_STEP[3] + 4:
                        act.wait_ge(proj_full, 6 * j + (6 + 4))
                        split(par % 2, V_, 16 * j + 48)

            pairs_loop(act, body)

        @block.vector
        def _(dve):
            def evac(par, jn, gi):
                kind, t = gi // 2, gi % 2
                cols = slice(t * HALF, (t + 1) * HALF)
                src = proj_ps[gi % 2]
                if kind == V_:
                    dve.wait_ge(proj_full, 6 * jn + (gi + 1))
                    nc.vector.tensor_copy(v_T[:, cols], src[:, :]).then_inc(proj_free, 1)
                    return
                dve.wait_ge(proj_hi, 8 * jn + (2 * (gi - 2) + 2))
                low, high = slice(0, HEAD), slice(HEAD, P)
                if kind == Q_:
                    for own, other, h in ((low, high, 0), (high, low, 1)):
                        last = nc.vector.scalar_tensor_tensor(
                            out=q_st[other, par, h, cols], in0=src[own, :], scalar=Q_SCALE,
                            in1=q_st[own, par, h, cols].bitcast(F32), op0=ALU.mult, op1=ALU.subtract)
                    last.then_inc(proj_free, 1)
                    return
                for own, h in ((low, 0), (high, 1)):
                    last = nc.vector.tensor_tensor(k_st[1][own, par, h, cols], src[own, :],
                                                   k_st[0][own, par, h, cols].bitcast(F32), ALU.subtract)
                last.then_inc(proj_free, 1)

            def turned_v(par, jn, t):
                dve.wait_ge(v_hi, 2 * jn + (t + 1))
                dst = v_cat[:, par, 4 * t:4 * t + 4, :, :, :]
                nc.vector.tensor_tensor(dst[:, :, :, 1, :], proj_ps[t][:, :].rearrange("p (g h d) -> p g h d", g=4, h=2),
                                        dst[:, :, :, 0, :].bitcast(F32), ALU.subtract).then_inc(v_lo, 1)

            def turned_tile(j, u):
                dve.wait_ge(turned_hi, UNITS * j + (u + 1))
                g = u % GROUPS
                for first, count in runs_of(g):
                    at = first - blocks_of(g)[0]
                    last = nc.vector.tensor_tensor(
                        pT_part(pT[1], g, first, count),
                        tile_ps[u % 2][:, at * P:(at + count) * P].rearrange("p (b q) -> p b q", b=count),
                        pT_part(pT[0], g, first, count).bitcast(F32), ALU.subtract)
                last.then_inc(turned_lo, 1)

            def add_bias(j, u):
                h, g = u // GROUPS, u % GROUPS
                n = P * len(blocks_of(g))
                table = bias_inner[:, h, :]
                if g == 0:
                    dve.wait_ge(bias_ready, 2 * j + (h + 1 + 2))
                    table = bias_full[:, h, P:NB]
                elif g == GROUPS - 1:
                    table = bias_full[:, h, 0:2 * P]
                dve.wait_ge(score_full, UNITS * j + (u + 1))
                dve.wait_ge(exp_done, UNITS * j + (u + 1))
                nc.vector.memset(spare[:, :], 0.0)
                nc.vector.tensor_tensor_reduce(out=score[:, u % 2, 0:n], in0=score_ps[u % 2][:, 0:n], in1=table,
                                               scale=-1.0, scalar=3e38, op0=ALU.add, op1=ALU.min,
                                               accum_out=nmax[:, u % 4:u % 4 + 1]).then_inc(score_done, 1)

            def normalise(j, u):
                n = P * len(blocks_of(u % GROUPS))
                dve.wait_ge(exp_done, UNITS * j + (u + 1 + 2))
                nc.vector.reciprocal(recip[:, u % 4:u % 4 + 1], total[:, u % 4:u % 4 + 1]).then_inc(recip_done, 1)
                dve.wait_ge(recip_done, UNITS * j + (u + 1))
                nc.vector.tensor_scalar(prob[:, u % 4, 0:n], prob[:, u % 4, 0:n], recip[:, u % 4:u % 4 + 1], None,
                                        ALU.mult).then_inc(prob_ready, 1)

            def out_sum(j, h, b):
                if h == 0 and b == 0:
                    dve.wait_ge(out_stored, 16 * j + 16)
                dve.wait_ge(low_done, 4 * j + (2 * h + b + 1))
                nc.vector.tensor_tensor(o_st[HEAD * h:HEAD * (h + 1), b * HALF:(b + 1) * HALF],
                                        out_ps[b][0:HEAD, :], o_low[0:HEAD, b, :], ALU.add).then_inc(out_done, 1)

            for credit, n in ((proj_free, 2), (score_done, 2), (turned_lo, 2), (out_done, 2)):
                dve.sem_inc(credit, n)
            for gi in (0, 1):
                evac(0, 0, gi)
            for t in range(2):
                turned_v(0, 0, t)
            for gi in range(2, 6):
                evac(0, 0, gi)

            def body(j, par, more, loads):
                for s in range(STEPS + 1):
                    if 1 <= s <= UNITS:
                        normalise(j, s - 1)
                    if more and s in EVAC_STEP[0:2]:
                        evac(1 - par, j + 1, EVAC_STEP.index(s))
                    if 3 <= s < UNITS + 3:
                        turned_tile(j, s - 3)
                    for h, b in out_evac_at(s):
                        out_sum(j, h, b)
                    if more and s - 1 in V_TURN_STEP:
                        turned_v(1 - par, j + 1, V_TURN_STEP.index(s - 1))
                    if s < UNITS:
                        add_bias(j, s)
                    if more and s in EVAC_STEP[2:]:
                        evac(1 - par, j + 1, EVAC_STEP.index(s))

            pairs_loop(dve, body)

        @block.tensor
        def _(pe):
            def project(par, jn, first, last):
                for m in range(first, last):
                    gi, i = divmod(m, GROUP_MMS)
                    kind, t = gi // 2, gi % 2
                    k, (wp, ap) = i // len(PASSES), PASSES[i % len(PASSES)]
                    if i == 0:
                        if t == 0:
                            pe.wait_ge(w_lo, 3 * jn + (kind + 1))
                        pe.wait_ge(proj_free, 6 * jn + (gi + 1))
                        if kind == K_:
                            pe.wait_ge(v_lo, 2 * jn + (t + 1))
                    mm = nc.tensor.matmul(proj_ps[gi % 2][:, :], w[wp][:, (par + kind) % 2, k, :],
                                          S.act[ap][:, k, t * HALF:(t + 1) * HALF],
                                          start=(i == 0), stop=(i == GROUP_MMS - 1))
                    if i == GROUP_MMS - 1:
                        mm.then_inc(proj_full, 1)

            def turn_v(jn, t):
                pe.wait_ge(proj_free, 6 * jn + (t + 1 + 2))
                for i in range(4):
                    mm = nc.tensor.transpose(proj_ps[t][:, i * P:(i + 1) * P],
                                             v_T[:, t * HALF + i * P:t * HALF + (i + 1) * P], S.ident[:, :])
                mm.then_inc(v_turned, 1)

            def turn_p(j, u):
                pe.wait_ge(prob_ready, UNITS * j + (u + 1))
                pe.wait_ge(turned_lo, UNITS * j + (u + 1))
                for i in range(len(blocks_of(u % GROUPS))):
                    mm = nc.tensor.transpose(tile_ps[u % 2][:, i * P:(i + 1) * P],
                                             prob[:, u % 4, i * P:(i + 1) * P], S.ident[:, :])
                mm.then_inc(turned, 1)

            def scores(par, j, u):
                h, g = u // GROUPS, u % GROUPS
                keys = blocks_of(g)
                cols = slice((g + keys[0]) * P, (g + keys[-1] + 1) * P)
                if u == 0:
                    pe.wait_ge(proj_free, 6 * j + (6 + 2))
                    pe.wait_ge(k_doubled, 64 * j + 64)
                pe.wait_ge(score_done, UNITS * j + (u + 1))
                for part in range(2):
                    mm = nc.tensor.matmul(score_ps[u % 2][:, 0:P * len(keys)], q_st[:, par, h, g * P:(g + 1) * P],
                                          k_st[part][:, par, h, cols], start=(part == 0), stop=(part == 1))
                mm.then_inc(score_full, 1)

            def weigh_v(par, j, h, k):
                u = GROUPS * h + min(k + 1, GROUPS - 1)
                pe.wait_ge(turned_lo, UNITS * j + (u + 1 + 2))
                if k == 0:
                    if h == 0:
                        pe.wait_ge(v_lo, 2 * j + 2)
                    pe.wait_ge(out_done, 4 * j + (2 * h + 1))
                if k == 3:
                    pe.wait_ge(out_done, 4 * j + (2 * h + 2))
                queries = [q for q in (k - 1, k, k + 1) if 0 <= q < GROUPS]
                for b in range(2):
                    mine = [q for q in queries if q // 4 == b]
                    if not mine:
                        continue
                    for part in range(2):
                        at = mine[0] - (k - 1)
                        mm = nc.tensor.matmul(
                            out_ps[b][:, (mine[0] - 4 * b) * P:(mine[-1] + 1 - 4 * b) * P],
                            v_cat[:, par, k, h, :, :].rearrange("p a d -> p (a d)"),
                            pT[part][:, k % 4, at * P:(at + len(mine)) * P],
                            start=(part == 0 and k == (0 if b == 0 else 3)),
                            stop=(part == 1 and k == (4 if b == 0 else 7)), skip_group_check=True)
                mm.then_inc(pv_done, 1)

            pe.sem_inc(pv_done, 3)
            project(0, 0, 0, 2 * GROUP_MMS)
            for t in range(2):
                turn_v(0, t)
            project(0, 0, 2 * GROUP_MMS, FILL)

            def body(j, par, more, loads):
                for s in range(STEPS):
                    if more and s < FILL_STEPS:
                        project(1 - par, j + 1, FILL * s // FILL_STEPS, FILL * (s + 1) // FILL_STEPS)
                    if s < UNITS:
                        scores(par, j, s)
                    if 2 <= s < UNITS + 2:
                        turn_p(j, s - 2)
                    for h, k in pv_units_at(s):
                        weigh_v(par, j, h, k)
                    if more and s in V_TURN_STEP:
                        turn_v(j + 1, V_TURN_STEP.index(s))

            pairs_loop(pe, body)


def load_rows(sp, S, slot, a, row, rows=1, cols=D, column=0):
    width = a.shape[-1]
    src = bass.AP(a.tensor, a.offset + row * width + column, [[width, P], [P * width, rows], [1, cols]])
    return sp.dma_start(S.raw[:, slot, :].rearrange("p (k n) -> p k n", k=rows), src)


def broadcast_row(a):
    return bass.AP(a.tensor, a.offset, [[0, P], [1, D]])


LN_STEPS = 6


def layer_norm_start(nc, dve, row, stats, mv, chain, at):
    for h in range(2):
        nc.vector.bn_stats(stats[:, h, :], row[:, h * HALF:(h + 1) * HALF]).then_inc(chain, 1)
    dve.wait_ge(chain, at + 2)
    nc.vector.memset(mv[:, 5:6], 0.0)
    nc.vector.bn_aggr(mv[:, 0:2], stats[:, :, :]).then_inc(chain, 1)
    dve.wait_ge(chain, at + 3)
    nc.vector.tensor_scalar_add(mv[:, 2:3], mv[:, 1:2], EPS).then_inc(chain, 1)


def layer_norm_finish(nc, dve, row, mv, gain, shift, chain, at, deviation, count):
    nc.vector.scalar_tensor_tensor(out=row, in0=row, scalar=mv[:, 0:1], in1=gain, op0=ALU.subtract, op1=ALU.mult)\
        .then_inc(chain, 1)
    dve.wait_ge(deviation, count)
    nc.vector.reciprocal(mv[:, 4:5], mv[:, 3:4]).then_inc(chain, 1)
    dve.wait_ge(chain, at + 6)
    return nc.vector.scalar_tensor_tensor(out=row, in0=row, scalar=mv[:, 4:5], in1=shift, op0=ALU.mult, op1=ALU.add)


def output_projection(nc, S, x, w_o, ln_g, ln_b, w_gate):
    with ExitStack() as ctx:
        def sb(name, shape, dt=F32):
            return ctx.enter_context(nc.sbuf_tensor(name, shape, dt))

        def sem(name):
            return ctx.enter_context(nc.semaphore(name))

        wo = [sb(f"w_o_{n}", [P, KC, D], F32R) for n in ("hi", "lo")]
        o_raw = sb("attention_tile", [P, 2, KC, P])
        o_part = [sb(f"attention_tile_{n}", [P, 2, KC, P], F32R) for n in ("hi", "lo")]
        xin = sb("x_tile", [P, 2, D])
        x1 = sb("x1_tile", [P, 2, D])
        gain, shift = sb("ln1_gain", [P, D]), sb("ln1_shift", [P, D])
        stats, mv = sb("ln1_stats", [P, 2, 2, 6]), sb("ln1_mean_var", [P, 2, 8])

        ln_in = sem("ln1_in")
        o_in = [sem(f"attention_tile_in{i}") for i in range(2)]
        x_in = [sem(f"x_tile_in{i}") for i in range(2)]
        wo_hi = sem("w_o_hi_done")
        wo_lo = sem("w_o_lo_done")
        o_hi = sem("attention_hi_done")
        o_lo = sem("attention_lo_done")
        y_full = sem("y_full")
        y_free = sem("y_free")
        chain = sem("ln1_chain")
        deviation = sem("ln1_deviation")
        x1_ready = sem("x1_ready")
        x1_stored = [sem(f"x1_stored{i}") for i in range(2)]
        turned = sem("x1_turned")
        turned_hi = sem("x1_T_hi_done")
        turned_lo = sem("x1_T_lo_done")
        block = ctx.enter_context(nc.Block())

        def x1_T_tile(par, q):
            return S.ps[4 + 2 * par + q][:, :].rearrange("p (i t) -> p i t", i=4)

        def tiles_loop(eng, body):
            body(0, 0, 0)
            with eng.Fori(0, GROUPS // 2 - 1) as it:
                body(2 * it + 1, 1, it)
                body(2 * it + 2, 0, it + 1)
            body(GROUPS - 1, 1, GROUPS // 2 - 1)

        @block.sync
        def _(sp):
            def value(v):
                return in_register(sp, v)

            def load(t, par):
                place, split, read = value(t * P), value(t + 1), value(2 * t + 2)
                place_x = value(t * (GC * D))
                sp.wait_ge(o_lo, split)
                sp.dma_start(o_raw[:, par, :, :], bass.AP(S.oT.tensor, place, [[T, P], [P * T, KC], [1, P]]))\
                  .then_inc(o_in[par], 16)
                sp.wait_ge(y_free, read)
                sp.dma_start(xin[:, par, :], bass.AP(x.tensor, place_x, [[GRID_W * D, ROWS], [D, GC], [1, D]]))\
                  .then_inc(x_in[par], 16)

            for i in range(2):
                sp.sem_inc(x1_stored[i], 16)
            load(0, 0)
            for n in range(4, KC):
                sp.wait_ge(wo_lo, n - 3)
                load_rows(sp, S, n % 4, w_o, n * P).then_inc(S.wo_in[n % 4], 16)
            sp.dma_start(gain[:, :], broadcast_row(ln_g)).then_inc(ln_in, 16)
            sp.dma_start(shift[:, :], broadcast_row(ln_b)).then_inc(ln_in, 16)

            def store(t, par):
                place, ready = value(t * (P * D)), value(t + 1)
                sp.wait_ge(x1_ready, ready)
                sp.dma_start(bass.AP(S.x1.tensor, place, [[D, P], [1, D]]), x1[:, par, :]).then_inc(x1_stored[par], 16)

            def body(t, par, nth):
                first, last = (isinstance(t, int) and t == n for n in (0, GROUPS - 1))
                if not last:
                    load(t + 1, 1 - par)
                if first:
                    for n in range(BLOCK_CHUNKS):
                        sp.wait_ge(wo_lo, KC - BLOCK_CHUNKS + n + 1)
                        load_gate(sp, S, w_gate, 0, n)
                else:
                    store(t - 1, 1 - par)
                if last:
                    store(t, par)

            tiles_loop(sp, body)
            for i in range(2):
                sp.wait_ge(x1_stored[i], 16 * (GROUPS // 2 + 1))

        @block.gpsimd
        def _(pool):
            pool.sem_inc(o_lo, 2)

            def split(t, par):
                pool.wait_ge(o_hi, t + 1)
                nc.gpsimd.tensor_tensor(o_part[1][:, par, :, :], o_raw[:, par, :, :],
                                        o_part[0][:, par, :, :].bitcast(F32), ALU.subtract).then_inc(o_lo, 1)

            split(0, 0)

            def body(t, par, nth):
                if not (isinstance(t, int) and t == GROUPS - 1):
                    split(t + 1, 1 - par)

            tiles_loop(pool, body)

        @block.scalar
        def _(act):
            def split(t, par, nth):
                act.wait_ge(o_in[par], 16 * nth + 16)
                act.wait_ge(y_full, 2 * t + 2)
                nc.scalar.activation(o_part[0][:, par, :, :], o_raw[:, par, :, :], ACT.Copy).then_inc(o_hi, 1)

            def turned_tile(t, par):
                for q in range(2):
                    act.wait_ge(turned, 2 * t + (q + 1))
                    nc.scalar.activation(S.act[0][:, 4 * q:4 * q + 4, bass.ds(t * P, P)], x1_T_tile(par, q),
                                         ACT.Copy).then_inc(turned_hi, 1)

            for n in range(KC):
                if n == 3:
                    split(0, 0, 0)
                act.wait_ge(S.wo_in[n % 4], 16 * (n // 4 + 1))
                nc.scalar.activation(wo[0][:, n, :], S.raw[:, n % 4, :], ACT.Copy).then_inc(wo_hi, 1)

            def body(t, par, nth):
                if not (isinstance(t, int) and t == GROUPS - 1):
                    split(t + 1, 1 - par, nth + par)
                act.wait_ge(chain, LN_STEPS * t + 4)
                nc.scalar.activation(mv[:, par, 3:4], mv[:, par, 2:3], ACT.Sqrt).then_inc(deviation, 1)
                if not (isinstance(t, int) and t == 0):
                    turned_tile(t - 1, 1 - par)
                if isinstance(t, int) and t == GROUPS - 1:
                    turned_tile(t, par)

            tiles_loop(act, body)

        @block.vector
        def _(dve):
            for credit, n in ((y_free, 4), (turned_lo, 4)):
                dve.sem_inc(credit, n)
            for n in range(KC):
                dve.wait_ge(wo_hi, n + 1)
                nc.vector.tensor_tensor(wo[1][:, n, :], S.raw[:, n % 4, :], wo[0][:, n, :].bitcast(F32),
                                        ALU.subtract).then_inc(wo_lo, 1)
            dve.wait_ge(ln_in, 32)

            def body(t, par, nth):
                row = x1[:, par, :]
                dve.wait_ge(x_in[par], 16 * nth + 16)
                dve.wait_ge(x1_stored[par], 16 * nth + 16)
                for h in range(2):
                    cols = slice(h * HALF, (h + 1) * HALF)
                    dve.wait_ge(y_full, 2 * t + (h + 1 + 4))
                    nc.vector.scalar_tensor_tensor(out=row[:, cols], in0=xin[:, par, cols], scalar=ALPHA,
                                                   in1=S.ps[2 * par + h][:, :], op0=ALU.mult, op1=ALU.add)\
                        .then_inc(y_free, 1)
                dve.wait_ge(y_free, 2 * t + (2 + 4))
                layer_norm_start(nc, dve, row, stats[:, par], mv[:, par], chain, LN_STEPS * t)
                layer_norm_finish(nc, dve, row, mv[:, par], gain[:, :], shift[:, :], chain, LN_STEPS * t,
                                  deviation, t + 1).then_inc(x1_ready, 1)
                if not (isinstance(t, int) and t == 0):
                    turned_tile(t - 1, 1 - par)
                if isinstance(t, int) and t == GROUPS - 1:
                    turned_tile(t, par)

            def turned_tile(t, par):
                for q in range(2):
                    dve.wait_ge(turned_hi, 2 * t + (q + 1))
                    nc.vector.tensor_tensor(S.act[1][:, 4 * q:4 * q + 4, bass.ds(t * P, P)], x1_T_tile(par, q),
                                            S.act[0][:, 4 * q:4 * q + 4, bass.ds(t * P, P)].bitcast(F32),
                                            ALU.subtract).then_inc(turned_lo, 1)

            tiles_loop(dve, body)

        @block.tensor
        def _(pe):
            pe.sem_inc(y_full, 4)

            def turn(t, par):
                pe.wait_ge(x1_ready, t + 1)
                for q in range(2):
                    pe.wait_ge(turned_lo, 2 * t + (q + 1))
                    for i in range(4):
                        k = 4 * q + i
                        mm = nc.tensor.transpose(S.ps[4 + 2 * par + q][:, i * P:(i + 1) * P],
                                                 x1[:, par, k * P:(k + 1) * P], S.ident[:, :])
                    mm.then_inc(turned, 1)

            def body(t, par, nth):
                first = isinstance(t, int) and t == 0
                pe.wait_ge(o_lo, t + (1 + 2))
                for h in range(2):
                    pe.wait_ge(y_free, 2 * t + (h + 1))
                for k in range(KC):
                    if first:
                        pe.wait_ge(wo_lo, k + 1)
                    for h in range(2):
                        for n, (wp, ap) in enumerate(PASSES):
                            mm = nc.tensor.matmul(S.ps[2 * par + h][:, :], o_part[ap][:, par, k, :],
                                                  wo[wp][:, k, h * HALF:(h + 1) * HALF],
                                                  start=(k == 0 and n == 0), stop=(k == KC - 1 and n == 2))
                        if k == KC - 1:
                            mm.then_inc(y_full, 1)
                if not first:
                    turn(t - 1, 1 - par)
                if isinstance(t, int) and t == GROUPS - 1:
                    turn(t, par)

            tiles_loop(pe, body)


BLOCK_CHUNKS = 4
BLOCKS = FF // (BLOCK_CHUNKS * P)
PC = PLE // P


def load_gate(sp, S, w_gate, half, i):
    load_rows(sp, S, i, w_gate, 2 * i * P, 2, HALF, half * HALF).then_inc(S.ff_in[i], 16)


def mlp(nc, S, p, w_ff1, w_ff2, ln_g, ln_b, w_gate, w_proj, out):
    with ExitStack() as ctx:
        def sb(name, shape, dt=F32):
            return ctx.enter_context(nc.sbuf_tensor(name, shape, dt))

        def sem(name):
            return ctx.enter_context(nc.semaphore(name))

        y = sb("y", [P, GROUPS, D])
        hid = [sb(f"hidden_T_{n}", [P, BLOCK_CHUNKS, T], F32R) for n in ("hi", "lo")]
        wb = [sb(f"w_ff2_{n}", [P, BLOCK_CHUNKS, D], F32R) for n in ("hi", "lo")]
        w1 = [sb(f"w_ff1_{n}", [P, 2, KC, P], F32R) for n in ("hi", "lo")]
        gated = sb("gated", [P, 2, HALF])
        relu = sb("relu", [P, 2, HALF])
        stats, mv = sb("ln2_stats", [P, 2, 2, 6]), sb("ln2_mean_var", [P, 2, 8])

        y_in = [sem(f"y_in{t}") for t in range(GROUPS)]
        w_hi = sem("mlp_w_hi_done")
        w_lo = sem("mlp_w_lo_done")
        p_turned = sem("p_turned")
        p_hi = sem("p_hi_done")
        p_lo = sem("p_lo_done")
        gate_full = sem("gate_full")
        ple_full = sem("ple_full")
        wg_used = sem("w_gate_chunk_used")
        sigmoid = sem("sigmoid_done")
        product = sem("product_done")
        gate_done = sem("gate_done")
        ff1_full = sem("ff1_full")
        relu_done = sem("relu_done")
        square = sem("square_done")
        hid_hi = sem("hidden_hi_done")
        hid_lo = sem("hidden_lo_done")
        ff2_full = sem("ff2_full")
        y_added = sem("y_added")
        ln_in = sem("ln2_in")
        chain = sem("ln2_chain")
        deviation = sem("ln2_deviation")
        out_ready = sem("out_ready")
        out_stored = sem("out_stored_final")
        block = ctx.enter_context(nc.Block())

        W_BLOCK = 2 + 8
        GROUPS1 = 2 * BLOCK_CHUNKS
        TILES2 = 2 * GROUPS

        def blocks_loop(eng, body):
            with eng.Fori(0, BLOCKS - 1) as b:
                body(b, False)
            body(BLOCKS - 1, True)

        @block.sync
        def _(sp):
            def value(v):
                return in_register(sp, v)

            def load_ff1(c, column):
                src = bass.AP(w_ff1.tensor, column, [[FF, P], [P * FF, KC], [1, P]])
                sp.dma_start(S.raw[:, c, :].rearrange("p (k n) -> p k n", k=KC), src).then_inc(S.ff_in[c], 16)

            for n in range(PC):
                sp.wait_ge(w_lo, n + 1)
                load_rows(sp, S, n, w_proj, n * P).then_inc(S.ff_in[n], 16)
            for n in range(2):
                sp.wait_ge(w_lo, 2 + n + 1)
                for i in range(4):
                    sp.dma_start(S.raw[:, 2 + n, i * PLE:(i + 1) * PLE], token_tile(p, 4 * n + i))\
                      .then_inc(S.ff_in[2 + n], 16)
            for t in range(GROUPS):
                sp.dma_start(y[:, t, :], S.x1[t]).then_inc(y_in[t], 16)
            for i in range(BLOCK_CHUNKS):
                if i < 2:
                    sp.wait_ge(w_lo, 4 + i + 1)
                else:
                    sp.wait_ge(p_turned, 2 * (i - 1))
                load_gate(sp, S, w_gate, 1, i)
            for c in range(BLOCK_CHUNKS):
                sp.wait_ge(w_lo, 2 + 4 + c + 1)
                load_ff1(c, c * P)

            def body(b, last):
                row = value(b * (BLOCK_CHUNKS * P * D))
                for c in range(BLOCK_CHUNKS):
                    place = value(row + c * P * D)
                    split = value(8 * b + (c + 4 + 7))
                    sp.wait_ge(w_lo, split)
                    sp.dma_start(S.raw[:, c, :], bass.AP(w_ff2.tensor, place, [[D, P], [1, D]]))\
                      .then_inc(S.ff_in[c], 16)
                if last:
                    for c, a in ((0, ln_g), (1, ln_b)):
                        sp.wait_ge(w_lo, 8 * BLOCKS + c + 7)
                        sp.dma_start(S.raw[:, c, :], broadcast_row(a)).then_inc(ln_in, 16)
                    return
                for c in range(BLOCK_CHUNKS):
                    place = value(b * (BLOCK_CHUNKS * P) + (BLOCK_CHUNKS + c) * P)
                    split = value(8 * b + (8 + c + 7))
                    sp.wait_ge(w_lo, split)
                    load_ff1(c, place)

            blocks_loop(sp, body)
            for t in range(GROUPS):
                sp.wait_ge(out_ready, t + 1)
                sp.dma_start(token_tile(out, t), y[:, t, :]).then_inc(out_stored, 16)
            sp.wait_ge(out_stored, 16 * GROUPS)

        EARLY = [(i, lambda part, i=i: wb[part][:, i, :]) for i in range(4)]
        EARLY += [(i, lambda part, i=i: hid[part][:, PC + i, :]) for i in range(PC)]
        EARLY += EARLY[:4]

        IN_BLOCK = [("ff1", 2), ("ff1", 3), ("ff2", 0), ("ff2", 1), ("ff2", 2), ("ff2", 3), ("ff1", 4), ("ff1", 5)]
        SPLIT_AFTER = [2, 4, 4, 5, 5, 6, 8, 8]

        def block_target(part, i):
            kind, c = IN_BLOCK[i]
            return (w1[part][:, c % 2, :, :].rearrange("p k n -> p (k n)") if kind == "ff1" else wb[part][:, c, :])

        @block.gpsimd
        def _(pool):
            def low(dst, hi, slot, count):
                pool.wait_ge(w_hi, count)
                nc.gpsimd.tensor_tensor(dst, S.raw[:, slot, :], hi.bitcast(F32), ALU.subtract).then_inc(w_lo, 1)

            pool.wait_ge(w_lo, W_BLOCK)
            for c in range(2):
                low(block_target(1, 6 + c), block_target(0, 6 + c), c, W_BLOCK + c + 1)

            def body(b, last):
                for i in range(GROUPS1 + 1):
                    for s, after in enumerate(SPLIT_AFTER):
                        if after == i and not (last and s >= 6):
                            low(block_target(1, s), block_target(0, s), IN_BLOCK[s][1] % 4, 8 * b + (W_BLOCK + 2 + s + 1))

            blocks_loop(pool, body)

        @block.scalar
        def _(act):
            def high(dst, slot, loads):
                act.wait_ge(S.ff_in[slot], loads)
                nc.scalar.activation(dst, S.raw[:, slot, :], ACT.Copy).then_inc(w_hi, 1)

            P_LOADS = (16, 16, 64, 64)
            for i in range(4):
                high(EARLY[i][1](0), i, 16)
            for i in range(PC):
                high(EARLY[4 + i][1](0), i, 32)
            for n in range(4):
                act.wait_ge(p_turned, n + 1)
                nc.scalar.activation(hid[0][:, n % 2, (n // 2) * HALF:(n // 2 + 1) * HALF], S.ps[4 + n][:, :],
                                     ACT.Copy).then_inc(p_hi, 1)

            def sigmoids(half):
                for t in range(GROUPS):
                    u = GROUPS * half + t
                    act.wait_ge(gate_full, u + 1)
                    act.wait_ge(gate_done, u + 1)
                    nc.scalar.activation(gated[:, u % 2, :], S.ps[u % 2][:, :], ACT.Sigmoid).then_inc(sigmoid, 1)

            sigmoids(0)
            for i in range(4):
                if i < 3:
                    act.wait_ge(wg_used, i + 1)
                high(EARLY[6 + i][1](0), i, P_LOADS[i] + 32)
            for c in range(2):
                high(block_target(0, 6 + c), c, P_LOADS[c] + 48)
            sigmoids(1)

            def body(b, last):
                for i in range(GROUPS1 + 1):
                    for s, after in enumerate(SPLIT_AFTER):
                        if after == i and not (last and s >= 6):
                            kind, c = IN_BLOCK[s]
                            if kind == "ff1" and s >= 6:
                                act.wait_ge(ff1_full, GROUPS1 * b + (4 + 2 * (c - 2) + 2))
                            loads = {0: 4, 1: 5}[0 if kind == "ff1" else 1] + (2 if c >= 4 else 0)
                            slot = c % 4
                            high(block_target(0, s), slot, 32 * b + (P_LOADS[slot] + 16 * (loads - 1)))
                    if i < GROUPS1:
                        act.wait_ge(ff1_full, GROUPS1 * b + (i + 1 + 4))
                        act.wait_ge(hid_lo, GROUPS1 * b + (i + 1 + 2))
                        nc.scalar.activation(relu[:, i % 2, :], S.ps[i % 4][:, :], ACT.Relu).then_inc(relu_done, 1)
                        act.wait_ge(square, GROUPS1 * b + (i + 1))
                        nc.scalar.activation(hid[0][:, i // 2, (i % 2) * HALF:(i % 2 + 1) * HALF], relu[:, i % 2, :],
                                             ACT.Copy).then_inc(hid_hi, 1)

            blocks_loop(act, body)
            for t in range(GROUPS):
                act.wait_ge(chain, LN_STEPS * t + 4)
                nc.scalar.activation(mv[:, t % 2, 3:4], mv[:, t % 2, 2:3], ACT.Sqrt).then_inc(deviation, 1)

        @block.vector
        def _(dve):
            for credit, n in ((gate_done, 2), (hid_lo, 4), (y_added, 4)):
                dve.sem_inc(credit, n)

            def low(m):
                slot, dst = EARLY[m]
                dve.wait_ge(w_hi, m + 1)
                nc.vector.tensor_tensor(dst(1), S.raw[:, slot, :], dst(0).bitcast(F32), ALU.subtract).then_inc(w_lo, 1)

            for m in range(6):
                low(m)
            for n in range(4):
                dve.wait_ge(p_hi, n + 1)
                cols = slice((n // 2) * HALF, (n // 2 + 1) * HALF)
                nc.vector.tensor_tensor(hid[1][:, n % 2, cols], S.ps[4 + n][:, :], hid[0][:, n % 2, cols].bitcast(F32),
                                        ALU.subtract).then_inc(p_lo, 1)
            for u in range(2 * GROUPS):
                half, t = divmod(u, GROUPS)
                cols = slice(half * HALF, (half + 1) * HALF)
                dve.wait_ge(sigmoid, u + 1)
                dve.wait_ge(ple_full, u + 1)
                nc.vector.tensor_tensor(gated[:, u % 2, :], gated[:, u % 2, :], S.ps[2 + u % 2][:, :], ALU.mult)\
                    .then_inc(product, 1)
                dve.wait_ge(y_in[t], 16)
                dve.wait_ge(product, u + 1)
                nc.vector.scalar_tensor_tensor(out=y[:, t, cols], in0=y[:, t, cols], scalar=ALPHA,
                                               in1=gated[:, u % 2, :], op0=ALU.mult, op1=ALU.add)\
                    .then_inc(gate_done, 1)
                if u == GROUPS - 1:
                    for m in range(6, W_BLOCK):
                        low(m)

            def body(b, last):
                for i in range(GROUPS1):
                    dve.wait_ge(relu_done, GROUPS1 * b + (i + 1))
                    nc.vector.tensor_tensor(relu[:, i % 2, :], relu[:, i % 2, :], relu[:, i % 2, :], ALU.mult)\
                        .then_inc(square, 1)
                    dve.wait_ge(hid_hi, GROUPS1 * b + (i + 1))
                    cols = slice((i % 2) * HALF, (i % 2 + 1) * HALF)
                    nc.vector.tensor_tensor(hid[1][:, i // 2, cols], relu[:, i % 2, :],
                                            hid[0][:, i // 2, cols].bitcast(F32), ALU.subtract).then_inc(hid_lo, 1)
                for n in range(TILES2):
                    t, h = divmod(n, 2)
                    cols = slice(h * HALF, (h + 1) * HALF)
                    dve.wait_ge(ff2_full, TILES2 * b + (n + 1))
                    nc.vector.tensor_tensor(y[:, t, cols], y[:, t, cols], S.ps[4 + n % 4][:, :], ALU.add)\
                        .then_inc(y_added, 1)
                    if last and h == 1:
                        if t == 0:
                            dve.wait_ge(ln_in, 32)
                        dve.wait_ge(y_added, TILES2 * b + (n + 1 + 4))
                        layer_norm_start(nc, dve, y[:, t, :], stats[:, t % 2], mv[:, t % 2], chain, LN_STEPS * t)
                        layer_norm_finish(nc, dve, y[:, t, :], mv[:, t % 2], S.raw[:, 0, :], S.raw[:, 1, :], chain,
                                          LN_STEPS * t, deviation, t + 1).then_inc(out_ready, 1)

            blocks_loop(dve, body)

        @block.tensor
        def _(pe):
            pe.sem_inc(ff1_full, 4)
            def gate_columns(part, k):
                return wb[part][:, k // 2, (k % 2) * HALF:(k % 2 + 1) * HALF]

            def gate(u):
                half, t = divmod(u, GROUPS)
                pe.wait_ge(gate_done, u + 1)
                for k in range(KC):
                    if t == 0 and k % 2 == 0:
                        pe.wait_ge(w_lo, 6 * half + k // 2 + 1)
                    for n, (wp, ap) in enumerate(PASSES):
                        mm = nc.tensor.matmul(S.ps[u % 2][:, :], S.act[ap][:, k, t * P:(t + 1) * P],
                                              gate_columns(wp, k), start=(k == 0 and n == 0),
                                              stop=(k == KC - 1 and n == 2))
                    if u == GROUPS - 1 and k % 2 and k < KC - 1:
                        mm.then_inc(wg_used, 1)
                mm.then_inc(gate_full, 1)

            def turn_p(n):
                c, th = n % 2, n // 2
                pe.wait_ge(S.ff_in[2 + th], 16 + 64)
                for i in range(4):
                    mm = nc.tensor.transpose(S.ps[4 + n][:, i * P:(i + 1) * P],
                                             S.raw[:, 2 + th, i * PLE + c * P:i * PLE + (c + 1) * P], S.ident[:, :])
                mm.then_inc(p_turned, 1)

            def embed(u):
                half, t = divmod(u, GROUPS)
                for k in range(PC):
                    for n, (wp, ap) in enumerate(PASSES):
                        mm = nc.tensor.matmul(S.ps[2 + u % 2][:, :], hid[ap][:, k, t * P:(t + 1) * P],
                                              hid[wp][:, PC + k, half * HALF:(half + 1) * HALF],
                                              start=(k == 0 and n == 0), stop=(k == PC - 1 and n == 2))
                mm.then_inc(ple_full, 1)

            gate(0)
            gate(1)
            for n in range(4):
                turn_p(n)
            pe.wait_ge(p_lo, 4)
            embed(0)
            embed(1)
            for u in range(2, 2 * GROUPS):
                gate(u)
                embed(u)
            pe.wait_ge(gate_done, 2 * GROUPS + 2)

            def body(b, last):
                for i in range(GROUPS1):
                    c, th = divmod(i, 2)
                    if th == 0:
                        pe.wait_ge(w_lo, 8 * b + (W_BLOCK + c + 1))
                    pe.wait_ge(hid_lo, GROUPS1 * b + (i + 1))
                    for k in range(KC):
                        for n, (wp, ap) in enumerate(PASSES):
                            mm = nc.tensor.matmul(S.ps[i % 4][:, :], w1[wp][:, c % 2, k, :],
                                                  S.act[ap][:, k, th * HALF:(th + 1) * HALF],
                                                  start=(k == 0 and n == 0), stop=(k == KC - 1 and n == 2))
                    mm.then_inc(ff1_full, 1)
                for n in range(TILES2):
                    t, h = divmod(n, 2)
                    if n == 0:
                        pe.wait_ge(w_lo, 8 * b + (W_BLOCK + 8))
                    if n in (0, TILES2 // 2):
                        pe.wait_ge(hid_lo, GROUPS1 * b + (GROUPS1 - 1 + (n > 0) + 4))
                    pe.wait_ge(y_added, TILES2 * b + (n + 1))
                    for k in range(BLOCK_CHUNKS):
                        for i, (wp, ap) in enumerate(PASSES):
                            mm = nc.tensor.matmul(S.ps[4 + n % 4][:, :], hid[ap][:, k, t * P:(t + 1) * P],
                                                  wb[wp][:, k, h * HALF:(h + 1) * HALF],
                                                  start=(k == 0 and i == 0), stop=(k == BLOCK_CHUNKS - 1 and i == 2))
                    mm.then_inc(ff2_full, 1)

            blocks_loop(pe, body)


INPUTS = ["x", "p", "na_w_qkv", "na_rpb", "na_w_o", "ln1_g", "ln1_b", "w_ff1", "w_ff2", "ln2_g", "ln2_b",
          "w_ple_gate", "w_ple_proj"]


def column_mask():
    query = np.arange(P) % GC
    key = np.arange(3 * GC).reshape(3, 1, GC)
    inside = (key[None] >= query[:, None, None, None]) & (key[None] < query[:, None, None, None] + KW)
    return np.broadcast_to(np.where(inside, 0.0, MASKED), (P, 3, ROWS, GC)).reshape(P, NB).astype(np.float32)


def kernel(**inputs):
    import concourse.bacc as bacc
    from concourse.bass_utils import run_bass_kernel_spmd

    nc = bacc.Bacc("TRN2", target_bir_lowering=False, num_devices=1)
    arrays = {f"in_{name}": np.ascontiguousarray(inputs[name]) for name in INPUTS}
    arrays["column_mask_table"] = column_mask()
    args = [nc.dram_tensor(name, a.shape, mybir.dt.from_np(a.dtype), kind="ExternalInput").ap()
            for name, a in arrays.items()]
    shape = inputs["x"].shape
    args.append(nc.dram_tensor("out", shape, F32, kind="ExternalOutput").ap())
    build_program(nc, *args)
    result = run_bass_kernel_spmd(nc, [arrays], core_ids=[0])
    return result.results[0]["out"]
```

```python
from contextlib import ExitStack

import numpy as np

import concourse.bass as bass
from concourse import mybir

P = 128
D = 1024
T = 1024
HEAD = 64
HEADS = D // HEAD
PAIRS = HEADS // 2
GRID_W = 64
ROWS = T // GRID_W
KH, KW = 8, 16
GC = 8
GROUPS = T // P
KC = D // P
HALF = 512
DR, DC = 2 * KH - 1, 2 * KW - 1
NB = 3 * P
FF = 4 * D
PLE = 256
PC = PLE // P
ALPHA = float(2 ** 0.25)
EPS = 1e-6
MASKED = -1e38

F32 = mybir.dt.float32
F32R = mybir.dt.float32r
ALU = mybir.AluOpType
ACT = mybir.ActivationFunctionType

V_, K_, Q_ = range(3)
W_COLUMN = {V_: 2 * D, K_: D, Q_: 0}
PASSES = ((0, 0), (0, 1), (1, 0))

UNITS = 2 * GROUPS
STEPS = UNITS + 4
GROUP_MMS = KC * len(PASSES)
FILL = 6 * GROUP_MMS
FILL_STEPS = STEPS - 1
EVAC_STEP = [(GROUP_MMS * (gi + 1) - 1) * FILL_STEPS // FILL + 1 for gi in range(6)]
V_TURN_STEP = (4, 7)
P_TURN_STEP = (0, 2)
EMBED_FROM = 4
WO_SPLIT_STEP = (7, 9)
FIRST_SPLIT_STEP = 13
FIRST_TILE_STEP = 4
RELOAD_STEP = (9, 12)


def blocks_of(g):
    return [d for d in (-1, 0, 1) if 0 <= g + d < GROUPS]


def runs_of(g):
    out = []
    for d in blocks_of(g):
        if out and (g + d) % 4:
            out[-1][1] += 1
        else:
            out.append([d, 1])
    return out


def pv_units_at(s):
    out = []
    for h in range(2):
        for k in range(GROUPS):
            if s == GROUPS * h + min(k + 1, GROUPS - 1) + 4:
                out.append((h, k))
    return out


def out_evac_at(s):
    return [(h, b) for h in range(2) for b in range(2) if s == GROUPS * h + (10 if b == 0 else 12)]


class Shared:
    pass


def build_program(nc, x, p, w_qkv, rpb, w_o, ln1_g, ln1_b, w_ff1, w_ff2, ln2_g, ln2_b, w_gate, w_proj, mask, out):
    with ExitStack() as ctx:
        S = Shared()
        S.raw = ctx.enter_context(nc.sbuf_tensor("weight_raw", [P, 4, D], F32))
        S.ident = ctx.enter_context(nc.sbuf_tensor("identity", [P, P], F32))
        S.act = [ctx.enter_context(nc.sbuf_tensor(f"act_T_{n}", [P, KC, T], F32R)) for n in ("hi", "lo")]
        S.ps = [ctx.enter_context(nc.psum_tensor(f"bank{i}", [P, HALF], F32)) for i in range(8)]
        S.oT = nc.dram_tensor("attention_T", [PAIRS, P, T], F32).ap()
        S.rpb_rows = nc.dram_tensor("rpb_rows", [GC, HEADS, DR, 3 * GC], F32).ap()
        S.rpb_stored = ctx.enter_context(nc.semaphore("rpb_rows_stored"))
        S.raw_in, S.wo_in, S.ff_in = ([ctx.enter_context(nc.semaphore(f"{n}_raw_in{i}")) for i in range(4)]
                                      for n in ("qkv", "w_o", "mlp"))
        S.x1 = nc.dram_tensor("x_after_attention", [GROUPS, P, D], F32).ap()
        S.embedded = nc.dram_tensor("ple_embedding", [GROUPS, P, D], F32).ap()
        S.out_stored = ctx.enter_context(nc.semaphore("out_stored"))
        S.embed_stored = [ctx.enter_context(nc.semaphore(f"embed_stored{i}")) for i in range(2)]
        S.wo_hi, S.wo_lo = (ctx.enter_context(nc.semaphore(f"w_o_{n}_done")) for n in ("hi", "lo"))
        S.first_in, S.first_hi, S.first_lo = (ctx.enter_context(nc.semaphore(f"attention_first_{n}"))
                                              for n in ("in", "hi_done", "lo_done"))
        S.x1_stored = [ctx.enter_context(nc.semaphore(f"x1_stored{i}")) for i in range(2)]
        with ExitStack() as first:
            S.w = [first.enter_context(nc.sbuf_tensor(f"w_qkv_{n}", [P, 2, KC, P], F32R)) for n in ("hi", "lo")]
            S.w_hi, S.w_lo = (first.enter_context(nc.semaphore(f"w_{n}_done")) for n in ("hi", "lo"))
            transpose_input(nc, S, x, w_qkv, rpb)
            attention(nc, S, w_qkv, mask, w_o, p, w_proj)
            output_projection(nc, S, x, w_o, ln1_g, ln1_b, w_gate)
        mlp(nc, S, w_ff1, w_ff2, ln2_g, ln2_b, w_gate, out)


def in_register(engine, v):
    return v if isinstance(v, int) else engine.snap(v)


def qkv_chunk(w_qkv, kind, offset):
    return bass.AP(w_qkv.tensor, w_qkv.offset + W_COLUMN[kind] + offset, [[3 * D, P], [P * 3 * D, KC], [1, P]])


def transpose_input(nc, S, x, w_qkv, rpb):
    with ExitStack() as ctx:
        xin = ctx.enter_context(nc.sbuf_tensor("x_tokens", [P, GROUPS, D], F32))
        x_in = [ctx.enter_context(nc.semaphore(f"x_in{g}")) for g in range(GROUPS)]
        zeroed = ctx.enter_context(nc.semaphore("identity_zeroed"))
        ident_ready = ctx.enter_context(nc.semaphore("identity_ready"))
        turned = ctx.enter_context(nc.semaphore("x_turned"))
        hi_done = ctx.enter_context(nc.semaphore("x_hi_done"))
        lo_done = ctx.enter_context(nc.semaphore("x_lo_done"))
        tiles = [(g, q) for g in range(GROUPS) for q in range(2)]
        block = ctx.enter_context(nc.Block())

        @block.sync
        def _(sp):
            for g in range(GROUPS):
                sp.dma_start(xin[:, g, :], token_tile(x, g)).then_inc(x_in[g], 16)
                if g in (1, 3, 5):
                    kind = g // 2
                    sp.dma_start(S.raw[:, kind, :].rearrange("p (k n) -> p k n", k=KC),
                                 qkv_chunk(w_qkv, kind, 0)).then_inc(S.raw_in[kind], 16)
            for c in range(GC):
                src = bass.AP(rpb.tensor, rpb.offset + KW - 1 - GC - c, [[DC, HEADS * DR], [1, 3 * GC]])
                sp.dma_start(S.rpb_rows[c].rearrange("h r w -> (h r) w"), src).then_inc(S.rpb_stored, 16)

        @block.gpsimd
        def _(pool):
            nc.gpsimd.memset(S.ident[:, :], 0.0).then_inc(zeroed, 1)
            pool.wait_ge(zeroed, 1)
            nc.gpsimd.affine_select(out=S.ident[:, :], in_=S.ident[:, :], compare_op=ALU.not_equal, fill=1.0,
                                    base=0, pattern=[[-1, P]], channel_multiplier=1).then_inc(ident_ready, 1)

        @block.tensor
        def _(pe):
            pe.wait_ge(ident_ready, 1)
            for n, (g, q) in enumerate(tiles):
                pe.wait_ge(x_in[g], 16)
                if n >= 8:
                    pe.wait_ge(lo_done, n - 7)
                for i in range(4):
                    k = 4 * q + i
                    last = nc.tensor.transpose(S.ps[n % 8][:, i * P:(i + 1) * P], xin[:, g, k * P:(k + 1) * P],
                                               S.ident[:, :])
                last.then_inc(turned, 1)

        def dest(part, g, q):
            return S.act[part][:, 4 * q:4 * q + 4, g * P:(g + 1) * P]

        def tile(n):
            return S.ps[n % 8][:, :].rearrange("p (i t) -> p i t", i=4)

        @block.scalar
        def _(act):
            for n, (g, q) in enumerate(tiles):
                act.wait_ge(turned, n + 1)
                nc.scalar.activation(dest(0, g, q), tile(n), ACT.Copy).then_inc(hi_done, 1)
            for kind in (V_, K_):
                act.wait_ge(S.raw_in[kind], 16)
                nc.scalar.activation(S.w[0][:, kind, :, :], S.raw[:, kind, :].rearrange("p (k n) -> p k n", k=KC),
                                     ACT.Copy).then_inc(S.w_hi, 1)

        @block.vector
        def _(dve):
            for n, (g, q) in enumerate(tiles):
                dve.wait_ge(hi_done, n + 1)
                nc.vector.tensor_tensor(dest(1, g, q), tile(n), dest(0, g, q).bitcast(F32),
                                        ALU.subtract).then_inc(lo_done, 1)
            for kind in (V_, K_):
                dve.wait_ge(S.w_hi, kind + 1)
                nc.vector.tensor_tensor(S.w[1][:, kind, :, :], S.raw[:, kind, :].rearrange("p (k n) -> p k n", k=KC),
                                        S.w[0][:, kind, :, :].bitcast(F32), ALU.subtract).then_inc(S.w_lo, 1)


def token_tile(a, g):
    width = a.shape[-1]
    return bass.AP(a.tensor, a.offset + g * GC * width, [[GRID_W * width, ROWS], [width, GC], [1, width]])


LAST = PAIRS - 1
EARLY_WO = 2


def early_w_o(S, part, n):
    return S.w[part][:, n, :, :].rearrange("p k n -> p (k n)")


def first_tile_raw(S):
    return S.act[0][:, 4, 0:LAST * P].bitcast(F32).rearrange("p (k t) -> p k t", k=LAST)


def first_tile(S, part):
    return S.act[part][:, 5, 0:LAST * P].rearrange("p (k t) -> p k t", k=LAST)


def attention(nc, S, w_qkv, mask, w_o, p, w_proj):
    with ExitStack() as ctx:
        def sb(name, shape, dt=F32):
            return ctx.enter_context(nc.sbuf_tensor(name, shape, dt))

        def sem(name):
            return ctx.enter_context(nc.semaphore(name))

        q_st = sb("q_hi_lo", [P, 2, 2, T], F32R)
        k_st = [sb(f"k_{n}_twice", [P, 2, 2, T], F32R) for n in ("hi", "lo")]
        v_T = sb("v_T", [P, T])
        v_cat = sb("v_hi_lo", [P, 2, GROUPS, 2, 2, HEAD], F32R)
        bias_in = sb("bias_in", [P, 2, ROWS, 3 * GC])
        bias_inner = sb("bias_inner", [P, 2, NB])
        bias_full = sb("bias_full", [P, 2, NB])
        col_mask = sb("column_mask", [P, NB])
        score = sb("negated_scores", [P, 2, NB])
        nmax = sb("negated_max", [P, 4])
        total = sb("exp_total", [P, 4])
        recip = sb("total_reciprocal", [P, 4])
        spare = sb("spare", [P, 1])
        prob = sb("probabilities", [P, 4, NB])
        pT = [sb(f"prob_T_{n}", [P, 4, NB], F32R) for n in ("hi", "lo")]
        o_low = sb("out_low_part", [P, 2, HALF])
        o_st = sb("out_T", [P, T])

        proj_full = sem("proj_full")
        proj_free = sem("proj_free")
        proj_hi = sem("proj_hi_done")
        bias_loaded = [sem(f"bias_loaded{h}") for h in range(2)]
        mask_loaded = sem("mask_loaded")
        bias_reset = sem("bias_reset")
        bias_ready = sem("bias_ready")
        score_full = sem("score_full")
        score_done = sem("score_done")
        exp_done = sem("exp_done")
        recip_done = sem("recip_done")
        prob_ready = sem("prob_ready")
        k_doubled = sem("k_doubled")
        v_turned = sem("v_turned")
        v_hi = sem("v_hi_done")
        v_lo = sem("v_lo_done")
        turned = sem("tile_turned")
        turned_hi = sem("tile_hi_done")
        turned_lo = sem("tile_lo_done")
        pv_done = sem("pv_done")
        low_done = sem("out_low_done")
        out_done = sem("out_done")
        out_stored, embed_stored = S.out_stored, S.embed_stored
        ple_in = [sem(f"ple_raw_in{i}") for i in range(4)]
        proj_w_hi = sem("w_proj_hi_done")
        proj_w_lo = sem("w_proj_lo_done")
        p_turned = sem("p_turned")
        p_hi = sem("p_hi_done")
        p_lo = sem("p_lo_done")
        embed_full = sem("embed_full")
        embed_out = sem("embed_out")
        block = ctx.enter_context(nc.Block())

        w, w_hi, w_lo = S.w, S.w_hi, S.w_lo
        proj_ps, score_ps, tile_ps, out_ps = S.ps[0:2], S.ps[2:4], S.ps[4:6], S.ps[6:8]
        Q_SCALE = HEAD ** -0.5

        def embed_place(u):
            return v_T[:, (u % 2) * HALF:(u % 2 + 1) * HALF]

        def pT_place(part, n):
            return S.act[part][:, PC + n % 2, (n // 2) * HALF:(n // 2 + 1) * HALF]

        def p_turns_at(s):
            return [2 * P_TURN_STEP.index(s) + i for i in range(2)] if s in P_TURN_STEP else []

        def pT_part(buf, g, first, count):
            slot = (g + first) % 4
            base = buf[:, slot, (1 - first) * P:(2 - first) * P]
            return bass.AP(base.tensor, base.offset, [list(base.ap[0]), [NB - P, count], [1, P]])

        def pairs_loop(eng, body):
            with eng.Fori(0, PAIRS // 2 - 1) as it:
                for par in range(2):
                    body(2 * it + par, par, True, True)
            body(PAIRS - 2, 0, True, False)
            body(PAIRS - 1, 1, False, False)

        @block.sync
        def _(sp):
            def value(v):
                return in_register(sp, v)

            def load_w(kind, offset):
                sp.dma_start(S.raw[:, kind, :].rearrange("p (k n) -> p k n", k=KC),
                             qkv_chunk(w_qkv, kind, offset)).then_inc(S.raw_in[kind], 16)

            def load_bias(h, offset, built):
                built = value(built)
                for qr in range(ROWS):
                    r0 = min(max(qr - KH // 2, 0), ROWS - KH)
                    start = value(offset + (r0 - qr + KH - 1) * 3 * GC)
                    if qr == 0:
                        sp.wait_ge(bias_ready, built)
                    src = bass.AP(S.rpb_rows.tensor, start, [[HEADS * DR * 3 * GC, GC], [1, KH * 3 * GC]])
                    sp.dma_start(bias_in[qr * GC:(qr + 1) * GC, h, r0:r0 + KH, :].rearrange("p r w -> p (r w)"), src)\
                      .then_inc(bias_loaded[h], 16)

            def k_twice(par, jn):
                written = value(6 * jn + (4 + 2))
                for h in range(2):
                    own, other = slice(HEAD * h, HEAD * (h + 1)), slice(HEAD * (1 - h), HEAD * (2 - h))
                    for part in range(2):
                        if h == 0 and part == 0:
                            sp.wait_ge(proj_free, written)
                        sp.dma_start(k_st[part][other, par, h, :].bitcast(F32),
                                     k_st[part][own, par, h, :].bitcast(F32)).then_inc(k_doubled, 16)

            sp.sem_inc(out_stored, 16)
            sp.dma_start(col_mask[:, :], mask).then_inc(mask_loaded, 16)
            sp.wait_ge(bias_reset, 1)
            sp.wait_ge(S.rpb_stored, 16 * GC)
            sp.sem_inc(bias_ready, 2)
            for h in range(2):
                load_bias(h, h * DR * 3 * GC, 2)
            for kind in range(3):
                sp.wait_ge(w_hi, kind + 1)
                sp.wait_ge(w_lo, kind + 1)
                load_w(kind, P)
            k_twice(0, 0)
            for h in range(2):
                load_bias(h, (2 + h) * DR * 3 * GC, h + 1 + 2)

            def body(j, par, more, loads):
                if loads:
                    column = value(j * P + 2 * P)
                    for kind in range(3):
                        split = value(3 * j + (3 + kind + 1))
                        sp.wait_ge(w_hi, split)
                        sp.wait_ge(w_lo, split)
                        load_w(kind, column)
                for h in range(2):
                    if loads:
                        load_bias(h, j * (2 * DR * 3 * GC) + (4 + h) * DR * 3 * GC, 2 * j + (2 + h + 1 + 2))
                    if more and not loads and h == 0:
                        sp.wait_ge(w_lo, 3 * PAIRS)
                        for n in range(PC):
                            load_rows(sp, S, n, w_proj, n * P).then_inc(ple_in[n], 16)
                        for n in range(2):
                            for i in range(4):
                                sp.dma_start(S.raw[:, 2 + n, i * PLE:(i + 1) * PLE], token_tile(p, 4 * n + i))\
                                  .then_inc(ple_in[2 + n], 16)
                    if more and h == 0:
                        k_twice(1 - par, j + 1)
                if not more:
                    for n in range(4):
                        if n < PC:
                            sp.wait_ge(proj_w_lo, n + 1)
                        else:
                            sp.wait_ge(p_turned, 2 * (n - 1))
                        load_rows(sp, S, n, w_o, n * P).then_inc(S.wo_in[n], 16)
                    for u in range(2 * GROUPS):
                        t, half = divmod(u, 2)
                        if u == FIRST_TILE_STEP:
                            sp.wait_ge(out_stored, 16 * PAIRS)
                            sp.dma_start(first_tile_raw(S), bass.AP(S.oT.tensor, 0, [[T, P], [P * T, LAST], [1, P]]))\
                              .then_inc(S.first_in, 16)
                        if u in RELOAD_STEP:
                            n = RELOAD_STEP.index(u)
                            sp.wait_ge(S.wo_lo, n + 1)
                            load_rows(sp, S, n, w_o, (4 + n) * P).then_inc(S.wo_in[n], 16)
                        sp.wait_ge(embed_out, u + 1)
                        sp.dma_start(S.embedded[t, :, half * HALF:(half + 1) * HALF], embed_place(u))\
                          .then_inc(embed_stored[half], 16)
                place, summed = value(j * (P * T)), value(4 * j + (4 + 2))
                sp.wait_ge(out_done, summed)
                sp.dma_start(bass.AP(S.oT.tensor, place, [[T, P], [1, T]]), o_st[:, :]).then_inc(out_stored, 16)

            pairs_loop(sp, body)

        @block.gpsimd
        def _(pool):
            nc.gpsimd.memset(bias_in[:, :, :, :], MASKED).then_inc(bias_reset, 1)
            pool.wait_ge(mask_loaded, 16)

            def split(slot, kind, count):
                pool.wait_ge(w_hi, count)
                nc.gpsimd.tensor_tensor(w[1][:, slot, :, :], S.raw[:, kind, :].rearrange("p (k n) -> p k n", k=KC),
                                        w[0][:, slot, :, :].bitcast(F32), ALU.subtract).then_inc(w_lo, 1)

            def build_bias(h, loads):
                pool.wait_ge(bias_loaded[h], loads)
                src = bias_in[:, h, :, :].rearrange("p r (d c) -> p d r c", d=3)
                shape = dict(d=3, r=ROWS)
                nc.gpsimd.tensor_tensor(bias_inner[:, h, :].rearrange("p (d r c) -> p d r c", **shape), src,
                                        col_mask[:, :].rearrange("p (d r c) -> p d r c", **shape), ALU.add)
                nc.gpsimd.tensor_copy(bias_full[:, h, :].rearrange("p (d r c) -> p d r c", **shape), src)\
                    .then_inc(bias_ready, 1)

            for h in range(2):
                build_bias(h, 16 * ROWS)
            split(0, Q_, 3)
            split(1, V_, 4)

            def body(j, par, more, loads):
                if more:
                    split((par + 1 + K_) % 2, K_, 3 * j + (3 + K_ + 1))
                    split((par + 1 + Q_) % 2, Q_, 3 * j + (3 + Q_ + 1))
                    pool.wait_ge(score_done, UNITS * j + (GROUPS + 2))
                    build_bias(0, 16 * ROWS * j + 2 * 16 * ROWS)
                if loads:
                    split(par % 2, V_, 3 * j + (6 + V_ + 1))
                if more:
                    pool.wait_ge(score_done, UNITS * j + (UNITS + 2))
                    build_bias(1, 16 * ROWS * j + 2 * 16 * ROWS)

                if not more:
                    for n in range(PC):
                        pool.wait_ge(proj_w_hi, n + 1)
                        nc.gpsimd.tensor_tensor(S.act[1][:, n, :], S.raw[:, n, :], S.act[0][:, n, :].bitcast(F32),
                                                ALU.subtract).then_inc(proj_w_lo, 1)
                    for n in range(EARLY_WO):
                        pool.wait_ge(S.wo_hi, n + 1)
                        nc.gpsimd.tensor_tensor(early_w_o(S, 1, n), S.raw[:, n, :], early_w_o(S, 0, n).bitcast(F32),
                                                ALU.subtract).then_inc(S.wo_lo, 1)
                    pool.wait_ge(S.first_hi, 1)
                    nc.gpsimd.tensor_tensor(first_tile(S, 1), first_tile_raw(S), first_tile(S, 0).bitcast(F32),
                                            ALU.subtract).then_inc(S.first_lo, 1)

            pairs_loop(pool, body)

        @block.scalar
        def _(act):
            def split(slot, kind, loads):
                act.wait_ge(S.raw_in[kind], loads)
                nc.scalar.activation(w[0][:, slot, :, :], S.raw[:, kind, :].rearrange("p (k n) -> p k n", k=KC),
                                     ACT.Copy).then_inc(w_hi, 1)

            def evac(par, jn, gi):
                kind, t = gi // 2, gi % 2
                if kind == V_:
                    return
                act.wait_ge(proj_full, 6 * jn + (gi + 1))
                dst = q_st if kind == Q_ else k_st[0]
                for h in range(2):
                    rows = slice(HEAD * h, HEAD * (h + 1))
                    nc.scalar.activation(dst[rows, par, h, t * HALF:(t + 1) * HALF], proj_ps[gi % 2][rows, :],
                                         ACT.Copy, scale=Q_SCALE if kind == Q_ else 1.0).then_inc(proj_hi, 1)

            def turned_v(par, jn, t):
                act.wait_ge(v_turned, 2 * jn + (t + 1))
                nc.scalar.activation(v_cat[:, par, 4 * t:4 * t + 4, :, 0, :],
                                     proj_ps[t][:, :].rearrange("p (g h d) -> p g h d", g=4, h=2),
                                     ACT.Copy).then_inc(v_hi, 1)

            def turned_tile(j, u):
                g = u % GROUPS
                act.wait_ge(turned, UNITS * j + (u + 1))
                act.wait_ge(pv_done, UNITS * j + (u + 1))
                for first, count in runs_of(g):
                    at = first - blocks_of(g)[0]
                    last = nc.scalar.activation(pT_part(pT[0], g, first, count),
                                                tile_ps[u % 2][:, at * P:(at + count) * P].rearrange(
                                                    "p (b q) -> p b q", b=count), ACT.Copy)
                last.then_inc(turned_hi, 1)

            def softmax_exp(j, u):
                g = u % GROUPS
                n = P * len(blocks_of(g))
                act.wait_ge(score_done, UNITS * j + (u + 1 + 2))
                nc.scalar.activation(prob[:, u % 4, 0:n], score[:, u % 2, 0:n], ACT.Exp, scale=-1.0,
                                     bias=nmax[:, u % 4:u % 4 + 1],
                                     accum_out=total[:, u % 4:u % 4 + 1]).then_inc(exp_done, 1)

            def out_low(j, h, b):
                act.wait_ge(pv_done, UNITS * j + (GROUPS * h + (5 if b == 0 else 8) + 3))
                act.wait_ge(out_done, 4 * j + (2 * h + b + 1))
                nc.scalar.activation(o_low[0:HEAD, b, :], out_ps[b][HEAD:P, :], ACT.Copy).then_inc(low_done, 1)

            def ple_work(s):
                if s < PC:
                    if s == 0:
                        act.wait_ge(proj_full, 6 * PAIRS)
                    act.wait_ge(ple_in[s], 16)
                    nc.scalar.activation(S.act[0][:, s, :], S.raw[:, s, :], ACT.Copy).then_inc(proj_w_hi, 1)
                if s in WO_SPLIT_STEP:
                    n = WO_SPLIT_STEP.index(s)
                    act.wait_ge(S.wo_in[n], 16)
                    nc.scalar.activation(early_w_o(S, 0, n), S.raw[:, n, :], ACT.Copy).then_inc(S.wo_hi, 1)
                if s == FIRST_SPLIT_STEP:
                    act.wait_ge(S.first_in, 16)
                    nc.scalar.activation(first_tile(S, 0), first_tile_raw(S), ACT.Copy).then_inc(S.first_hi, 1)
                if s - 1 in P_TURN_STEP:
                    for n in p_turns_at(s - 1):
                        act.wait_ge(p_turned, n + 1)
                        nc.scalar.activation(pT_place(0, n), proj_ps[n % 2][:, :], ACT.Copy).then_inc(p_hi, 1)
                if 0 <= s - 1 - EMBED_FROM < 2 * GROUPS:
                    u = s - 1 - EMBED_FROM
                    act.wait_ge(embed_full, u + 1)
                    if u >= 2:
                        act.wait_ge(embed_stored[u % 2], 16 * (u // 2))
                    nc.scalar.activation(embed_place(u), proj_ps[u % 2][:, :], ACT.Copy).then_inc(embed_out, 1)

            act.sem_inc(exp_done, 2)
            act.wait_ge(proj_full, 2)
            split(0, Q_, 16)
            for t in range(2):
                turned_v(0, 0, t)
            for gi in (2, 3):
                evac(0, 0, gi)
            split(1, V_, 32)
            for gi in (4, 5):
                evac(0, 0, gi)

            def body(j, par, more, loads):
                for s in range(STEPS + 1):
                    if 3 <= s < UNITS + 3:
                        turned_tile(j, s - 3)
                    for h, b in out_evac_at(s):
                        out_low(j, h, b)
                    if more and s in EVAC_STEP[2:]:
                        evac(1 - par, j + 1, EVAC_STEP.index(s))
                    if more and s - 1 in V_TURN_STEP:
                        turned_v(1 - par, j + 1, V_TURN_STEP.index(s - 1))
                    if not more:
                        ple_work(s)
                    if s < UNITS:
                        softmax_exp(j, s)
                    if not more:
                        continue
                    if s == 1:
                        split((par + 1 + K_) % 2, K_, 16 * j + 32)
                    if s == EVAC_STEP[1] + 2:
                        act.wait_ge(proj_full, 6 * j + (6 + 2))
                        split((par + 1 + Q_) % 2, Q_, 16 * j + 32)
                    if loads and s == EVAC_STEP[3] + 4:
                        act.wait_ge(proj_full, 6 * j + (6 + 4))
                        split(par % 2, V_, 16 * j + 48)

            pairs_loop(act, body)

        @block.vector
        def _(dve):
            def evac(par, jn, gi):
                kind, t = gi // 2, gi % 2
                cols = slice(t * HALF, (t + 1) * HALF)
                src = proj_ps[gi % 2]
                if kind == V_:
                    dve.wait_ge(proj_full, 6 * jn + (gi + 1))
                    nc.vector.tensor_copy(v_T[:, cols], src[:, :]).then_inc(proj_free, 1)
                    return
                dve.wait_ge(proj_hi, 8 * jn + (2 * (gi - 2) + 2))
                low, high = slice(0, HEAD), slice(HEAD, P)
                if kind == Q_:
                    for own, other, h in ((low, high, 0), (high, low, 1)):
                        last = nc.vector.scalar_tensor_tensor(
                            out=q_st[other, par, h, cols], in0=src[own, :], scalar=Q_SCALE,
                            in1=q_st[own, par, h, cols].bitcast(F32), op0=ALU.mult, op1=ALU.subtract)
                    last.then_inc(proj_free, 1)
                    return
                for own, h in ((low, 0), (high, 1)):
                    last = nc.vector.tensor_tensor(k_st[1][own, par, h, cols], src[own, :],
                                                   k_st[0][own, par, h, cols].bitcast(F32), ALU.subtract)
                last.then_inc(proj_free, 1)

            def turned_v(par, jn, t):
                dve.wait_ge(v_hi, 2 * jn + (t + 1))
                dst = v_cat[:, par, 4 * t:4 * t + 4, :, :, :]
                nc.vector.tensor_tensor(dst[:, :, :, 1, :], proj_ps[t][:, :].rearrange("p (g h d) -> p g h d", g=4, h=2),
                                        dst[:, :, :, 0, :].bitcast(F32), ALU.subtract).then_inc(v_lo, 1)

            def turned_tile(j, u):
                dve.wait_ge(turned_hi, UNITS * j + (u + 1))
                g = u % GROUPS
                for first, count in runs_of(g):
                    at = first - blocks_of(g)[0]
                    last = nc.vector.tensor_tensor(
                        pT_part(pT[1], g, first, count),
                        tile_ps[u % 2][:, at * P:(at + count) * P].rearrange("p (b q) -> p b q", b=count),
                        pT_part(pT[0], g, first, count).bitcast(F32), ALU.subtract)
                last.then_inc(turned_lo, 1)

            def add_bias(j, u):
                h, g = u // GROUPS, u % GROUPS
                n = P * len(blocks_of(g))
                table = bias_inner[:, h, :]
                if g == 0:
                    dve.wait_ge(bias_ready, 2 * j + (h + 1 + 2))
                    table = bias_full[:, h, P:NB]
                elif g == GROUPS - 1:
                    table = bias_full[:, h, 0:2 * P]
                dve.wait_ge(score_full, UNITS * j + (u + 1))
                dve.wait_ge(exp_done, UNITS * j + (u + 1))
                nc.vector.memset(spare[:, :], 0.0)
                nc.vector.tensor_tensor_reduce(out=score[:, u % 2, 0:n], in0=score_ps[u % 2][:, 0:n], in1=table,
                                               scale=-1.0, scalar=3e38, op0=ALU.add, op1=ALU.min,
                                               accum_out=nmax[:, u % 4:u % 4 + 1]).then_inc(score_done, 1)

            def normalise(j, u):
                n = P * len(blocks_of(u % GROUPS))
                dve.wait_ge(exp_done, UNITS * j + (u + 1 + 2))
                nc.vector.reciprocal(recip[:, u % 4:u % 4 + 1], total[:, u % 4:u % 4 + 1]).then_inc(recip_done, 1)
                dve.wait_ge(recip_done, UNITS * j + (u + 1))
                nc.vector.tensor_scalar(prob[:, u % 4, 0:n], prob[:, u % 4, 0:n], recip[:, u % 4:u % 4 + 1], None,
                                        ALU.mult).then_inc(prob_ready, 1)

            def out_sum(j, h, b):
                if h == 0 and b == 0:
                    dve.wait_ge(out_stored, 16 * j + 16)
                dve.wait_ge(low_done, 4 * j + (2 * h + b + 1))
                nc.vector.tensor_tensor(o_st[HEAD * h:HEAD * (h + 1), b * HALF:(b + 1) * HALF],
                                        out_ps[b][0:HEAD, :], o_low[0:HEAD, b, :], ALU.add).then_inc(out_done, 1)

            for credit, n in ((proj_free, 2), (score_done, 2), (turned_lo, 2), (out_done, 2)):
                dve.sem_inc(credit, n)
            for gi in (0, 1):
                evac(0, 0, gi)
            for t in range(2):
                turned_v(0, 0, t)
            for gi in range(2, 6):
                evac(0, 0, gi)

            def body(j, par, more, loads):
                for s in range(STEPS + 1):
                    if 1 <= s <= UNITS:
                        normalise(j, s - 1)
                    if more and s in EVAC_STEP[0:2]:
                        evac(1 - par, j + 1, EVAC_STEP.index(s))
                    if 3 <= s < UNITS + 3:
                        turned_tile(j, s - 3)
                    for h, b in out_evac_at(s):
                        out_sum(j, h, b)
                    if more and s - 1 in V_TURN_STEP:
                        turned_v(1 - par, j + 1, V_TURN_STEP.index(s - 1))
                    if not more:
                        for n in p_turns_at(s - 1):
                            dve.wait_ge(p_hi, n + 1)
                            nc.vector.tensor_tensor(pT_place(1, n), proj_ps[n % 2][:, :], pT_place(0, n).bitcast(F32),
                                                    ALU.subtract).then_inc(p_lo, 1)
                    if s < UNITS:
                        add_bias(j, s)
                    if more and s in EVAC_STEP[2:]:
                        evac(1 - par, j + 1, EVAC_STEP.index(s))

            pairs_loop(dve, body)

        @block.tensor
        def _(pe):
            def project(par, jn, first, last):
                for m in range(first, last):
                    gi, i = divmod(m, GROUP_MMS)
                    kind, t = gi // 2, gi % 2
                    k, (wp, ap) = i // len(PASSES), PASSES[i % len(PASSES)]
                    if i == 0:
                        if t == 0:
                            pe.wait_ge(w_lo, 3 * jn + (kind + 1))
                        pe.wait_ge(proj_free, 6 * jn + (gi + 1))
                        if kind == K_:
                            pe.wait_ge(v_lo, 2 * jn + (t + 1))
                    mm = nc.tensor.matmul(proj_ps[gi % 2][:, :], w[wp][:, (par + kind) % 2, k, :],
                                          S.act[ap][:, k, t * HALF:(t + 1) * HALF],
                                          start=(i == 0), stop=(i == GROUP_MMS - 1))
                    if i == GROUP_MMS - 1:
                        mm.then_inc(proj_full, 1)

            def turn_v(jn, t):
                pe.wait_ge(proj_free, 6 * jn + (t + 1 + 2))
                for i in range(4):
                    mm = nc.tensor.transpose(proj_ps[t][:, i * P:(i + 1) * P],
                                             v_T[:, t * HALF + i * P:t * HALF + (i + 1) * P], S.ident[:, :])
                mm.then_inc(v_turned, 1)

            def turn_p(j, u):
                pe.wait_ge(prob_ready, UNITS * j + (u + 1))
                pe.wait_ge(turned_lo, UNITS * j + (u + 1))
                for i in range(len(blocks_of(u % GROUPS))):
                    mm = nc.tensor.transpose(tile_ps[u % 2][:, i * P:(i + 1) * P],
                                             prob[:, u % 4, i * P:(i + 1) * P], S.ident[:, :])
                mm.then_inc(turned, 1)

            def scores(par, j, u):
                h, g = u // GROUPS, u % GROUPS
                keys = blocks_of(g)
                cols = slice((g + keys[0]) * P, (g + keys[-1] + 1) * P)
                if u == 0:
                    pe.wait_ge(proj_free, 6 * j + (6 + 2))
                    pe.wait_ge(k_doubled, 64 * j + 64)
                pe.wait_ge(score_done, UNITS * j + (u + 1))
                for part in range(2):
                    mm = nc.tensor.matmul(score_ps[u % 2][:, 0:P * len(keys)], q_st[:, par, h, g * P:(g + 1) * P],
                                          k_st[part][:, par, h, cols], start=(part == 0), stop=(part == 1))
                mm.then_inc(score_full, 1)

            def weigh_v(par, j, h, k):
                u = GROUPS * h + min(k + 1, GROUPS - 1)
                pe.wait_ge(turned_lo, UNITS * j + (u + 1 + 2))
                if k == 0:
                    if h == 0:
                        pe.wait_ge(v_lo, 2 * j + 2)
                    pe.wait_ge(out_done, 4 * j + (2 * h + 1))
                if k == 3:
                    pe.wait_ge(out_done, 4 * j + (2 * h + 2))
                queries = [q for q in (k - 1, k, k + 1) if 0 <= q < GROUPS]
                for b in range(2):
                    mine = [q for q in queries if q // 4 == b]
                    if not mine:
                        continue
                    for part in range(2):
                        at = mine[0] - (k - 1)
                        mm = nc.tensor.matmul(
                            out_ps[b][:, (mine[0] - 4 * b) * P:(mine[-1] + 1 - 4 * b) * P],
                            v_cat[:, par, k, h, :, :].rearrange("p a d -> p (a d)"),
                            pT[part][:, k % 4, at * P:(at + len(mine)) * P],
                            start=(part == 0 and k == (0 if b == 0 else 3)),
                            stop=(part == 1 and k == (4 if b == 0 else 7)), skip_group_check=True)
                mm.then_inc(pv_done, 1)

            def turn_p_rows(n):
                c, th = n % 2, n // 2
                pe.wait_ge(ple_in[2 + th], 64)
                if n >= 2:
                    pe.wait_ge(p_lo, n - 1)
                for i in range(4):
                    mm = nc.tensor.transpose(proj_ps[n % 2][:, i * P:(i + 1) * P],
                                             S.raw[:, 2 + th, i * PLE + c * P:i * PLE + (c + 1) * P], S.ident[:, :])
                mm.then_inc(p_turned, 1)

            def embed(u):
                t, half = divmod(u, 2)
                if u < 2:
                    pe.wait_ge(p_lo, 2 * len(P_TURN_STEP))
                else:
                    pe.wait_ge(embed_out, u - 1)
                for k in range(PC):
                    if u == 0:
                        pe.wait_ge(proj_w_lo, k + 1)
                    for n, (wp, ap) in enumerate(PASSES):
                        mm = nc.tensor.matmul(proj_ps[u % 2][:, :], S.act[ap][:, PC + k, t * P:(t + 1) * P],
                                              S.act[wp][:, k, half * HALF:(half + 1) * HALF],
                                              start=(k == 0 and n == 0), stop=(k == PC - 1 and n == 2))
                mm.then_inc(embed_full, 1)

            pe.sem_inc(pv_done, 3)
            project(0, 0, 0, 2 * GROUP_MMS)
            for t in range(2):
                turn_v(0, t)
            project(0, 0, 2 * GROUP_MMS, FILL)

            def body(j, par, more, loads):
                for s in range(STEPS):
                    if more and s < FILL_STEPS:
                        project(1 - par, j + 1, FILL * s // FILL_STEPS, FILL * (s + 1) // FILL_STEPS)
                    if s < UNITS:
                        scores(par, j, s)
                    if not more and 0 <= s - EMBED_FROM < 2 * GROUPS:
                        embed(s - EMBED_FROM)
                    if 2 <= s < UNITS + 2:
                        turn_p(j, s - 2)
                    for h, k in pv_units_at(s):
                        weigh_v(par, j, h, k)
                    if more and s in V_TURN_STEP:
                        turn_v(j + 1, V_TURN_STEP.index(s))
                    if not more:
                        for n in p_turns_at(s):
                            turn_p_rows(n)

            pairs_loop(pe, body)


def load_rows(sp, S, slot, a, row, rows=1, cols=D, column=0):
    width = a.shape[-1]
    src = bass.AP(a.tensor, a.offset + row * width + column, [[width, P], [P * width, rows], [1, cols]])
    return sp.dma_start(S.raw[:, slot, :].rearrange("p (k n) -> p k n", k=rows), src)


def broadcast_row(a):
    return bass.AP(a.tensor, a.offset, [[0, P], [1, D]])


LN_STEPS = 6


def half_statistics(nc, row, stats, h, chain):
    nc.vector.bn_stats(stats[:, h, :], row[:, h * HALF:(h + 1) * HALF]).then_inc(chain, 1)


def layer_norm_start(nc, dve, stats, mv, chain, at):
    dve.wait_ge(chain, at + 2)
    nc.vector.memset(mv[:, 5:6], 0.0)
    nc.vector.bn_aggr(mv[:, 0:2], stats[:, :, :]).then_inc(chain, 1)
    dve.wait_ge(chain, at + 3)
    nc.vector.tensor_scalar_add(mv[:, 2:3], mv[:, 1:2], EPS).then_inc(chain, 1)


def layer_norm_finish(nc, dve, row, mv, gain, shift, chain, at, deviation, count, ready):
    nc.vector.scalar_tensor_tensor(out=row, in0=row, scalar=mv[:, 0:1], in1=gain, op0=ALU.subtract, op1=ALU.mult)\
        .then_inc(chain, 1)
    dve.wait_ge(deviation, count)
    nc.vector.reciprocal(mv[:, 4:5], mv[:, 3:4]).then_inc(chain, 1)
    dve.wait_ge(chain, at + 6)
    for h in range(2):
        cols = slice(h * HALF, (h + 1) * HALF)
        nc.vector.scalar_tensor_tensor(out=row[:, cols], in0=row[:, cols], scalar=mv[:, 4:5], in1=shift[:, cols],
                                       op0=ALU.mult, op1=ALU.add).then_inc(ready, 1)


def output_projection(nc, S, x, w_o, ln_g, ln_b, w_gate):
    with ExitStack() as ctx:
        def sb(name, shape, dt=F32):
            return ctx.enter_context(nc.sbuf_tensor(name, shape, dt))

        def sem(name):
            return ctx.enter_context(nc.semaphore(name))

        late = [sb(f"w_o_{n}", [P, KC - EARLY_WO, D], F32R) for n in ("hi", "lo")]
        xin = sb("x_tile", [P, 2, D])
        o_raw = sb("attention_tile", [P, 2, KC, P])
        o_part = [sb(f"attention_tile_{n}", [P, 2, KC, P], F32R) for n in ("hi", "lo")]
        x1 = sb("x1_tile", [P, 2, D])
        gain, shift = sb("ln1_gain", [P, D]), sb("ln1_shift", [P, D])
        stats, mv = sb("ln1_stats", [P, 2, 2, 6]), sb("ln1_mean_var", [P, 2, 8])

        ln_in = sem("ln1_in")
        o_in = [sem(f"attention_tile_in{i}") for i in range(2)]
        x_in = [sem(f"x_tile_in{i}") for i in range(2)]
        wo_hi, wo_lo = S.wo_hi, S.wo_lo
        o_hi = sem("attention_hi_done")
        o_lo = sem("attention_lo_done")
        last_in = sem("attention_last_pair_in")
        y_full = sem("y_full")
        y_free = sem("y_free")
        chain = sem("ln1_chain")
        deviation = sem("ln1_deviation")
        x1_ready = sem("x1_ready")
        x1_stored = S.x1_stored
        turned = sem("x1_turned")
        turned_hi = sem("x1_T_hi_done")
        turned_lo = sem("x1_T_lo_done")
        block = ctx.enter_context(nc.Block())

        def wo(part, n):
            return early_w_o(S, part, n) if n < EARLY_WO else late[part][:, n - EARLY_WO, :]

        def x1_T_tile(par, q):
            return S.ps[4 + 2 * par + q][:, :].rearrange("p (i t) -> p i t", i=4)

        def tiles_loop(eng, body):
            body(0, 0, 0)
            with eng.Fori(0, GROUPS // 2 - 1) as it:
                body(2 * it + 1, 1, it)
                body(2 * it + 2, 0, it + 1)
            body(GROUPS - 1, 1, GROUPS // 2 - 1)

        @block.sync
        def _(sp):
            def value(v):
                return in_register(sp, v)

            def load_attention(t, par):
                place, split = value(t * P), value(t + 1)
                if not (isinstance(t, int) and t == 1):
                    sp.wait_ge(o_lo, split)
                sp.dma_start(o_raw[:, par, :, :], bass.AP(S.oT.tensor, place, [[T, P], [P * T, KC], [1, P]]))\
                  .then_inc(o_in[par], 16)

            def load_x(t, par):
                place_x, read = value(t * (GC * D)), value(2 * t + 2)
                sp.wait_ge(y_free, read)
                sp.dma_start(xin[:, par, :], bass.AP(x.tensor, place_x, [[GRID_W * D, ROWS], [D, GC], [1, D]]))\
                  .then_inc(x_in[par], 16)

            for i in range(2):
                sp.sem_inc(x1_stored[i], 16)
            for n in range(4 + EARLY_WO, KC):
                if n == KC - 1:
                    sp.wait_ge(S.out_stored, 16 * (PAIRS + 1))
                    sp.dma_start(o_raw[:, 0, LAST, :], bass.AP(S.oT.tensor, LAST * P * T, [[T, P], [1, P]]))\
                      .then_inc(last_in, 16)
                sp.wait_ge(wo_lo, n - 3)
                load_rows(sp, S, n % 4, w_o, n * P).then_inc(S.wo_in[n % 4], 16)
            load_attention(1, 1)
            for i in range(2):
                sp.wait_ge(S.embed_stored[i], 16 * GROUPS)
            sp.dma_start(xin[:, 0, :], bass.AP(x.tensor, 0, [[GRID_W * D, ROWS], [D, GC], [1, D]]))\
              .then_inc(x_in[0], 16)
            sp.dma_start(gain[:, :], broadcast_row(ln_g)).then_inc(ln_in, 16)
            sp.dma_start(shift[:, :], broadcast_row(ln_b)).then_inc(ln_in, 16)

            def store(t, par):
                place, ready = value(t * (P * D)), value(2 * t + 2)
                sp.wait_ge(x1_ready, ready)
                sp.dma_start(bass.AP(S.x1.tensor, place, [[D, P], [1, D]]), x1[:, par, :]).then_inc(x1_stored[par], 16)

            def body(t, par, nth):
                first, last = (isinstance(t, int) and t == n for n in (0, GROUPS - 1))
                if not last:
                    if not first:
                        load_attention(t + 1, 1 - par)
                    load_x(t + 1, 1 - par)
                if last:
                    sp.wait_ge(wo_lo, KC)
                    for n in range(BLOCK_CHUNKS):
                        load_gate(sp, S, w_gate, 0, n)
                if not first:
                    store(t - 1, 1 - par)
                if last:
                    store(t, par)

            tiles_loop(sp, body)

        @block.gpsimd
        def _(pool):

            def split(t, par):
                pool.wait_ge(o_hi, t + 1)
                nc.gpsimd.tensor_tensor(o_part[1][:, par, :, :], o_raw[:, par, :, :],
                                        o_part[0][:, par, :, :].bitcast(F32), ALU.subtract).then_inc(o_lo, 1)

            pool.wait_ge(o_lo, 1 + 2)

            def body(t, par, nth):
                if not (isinstance(t, int) and t == GROUPS - 1):
                    split(t + 1, 1 - par)

            tiles_loop(pool, body)

        @block.scalar
        def _(act):
            def split(t, par, nth):
                act.wait_ge(o_in[par], 16 * nth + 16 * par)
                act.wait_ge(y_full, 2 * t + 2)
                nc.scalar.activation(o_part[0][:, par, :, :], o_raw[:, par, :, :], ACT.Copy).then_inc(o_hi, 1)

            def turned_tile(t, par):
                for q in range(2):
                    act.wait_ge(turned, 2 * t + (q + 1))
                    nc.scalar.activation(S.act[0][:, 4 * q:4 * q + 4, bass.ds(t * P, P)], x1_T_tile(par, q),
                                         ACT.Copy).then_inc(turned_hi, 1)

            for n in range(EARLY_WO, KC):
                if n == 6:
                    act.wait_ge(last_in, 16)
                    nc.scalar.activation(o_part[0][:, 0, LAST, :], o_raw[:, 0, LAST, :], ACT.Copy).then_inc(o_hi, 1)
                if n == 7:
                    split(1, 1, 0)
                act.wait_ge(S.wo_in[n % 4], 16 * (n // 4 + 1))
                nc.scalar.activation(wo(0, n), S.raw[:, n % 4, :], ACT.Copy).then_inc(wo_hi, 1)

            def body(t, par, nth):
                if not (isinstance(t, int) and t in (0, GROUPS - 1)):
                    split(t + 1, 1 - par, nth + par)
                act.wait_ge(chain, LN_STEPS * t + 4)
                nc.scalar.activation(mv[:, par, 3:4], mv[:, par, 2:3], ACT.Sqrt).then_inc(deviation, 1)
                if not (isinstance(t, int) and t == 0):
                    turned_tile(t - 1, 1 - par)
                if isinstance(t, int) and t == GROUPS - 1:
                    turned_tile(t, par)

            tiles_loop(act, body)

        @block.vector
        def _(dve):
            for credit, n in ((y_free, 4), (turned_lo, 4), (o_lo, 2)):
                dve.sem_inc(credit, n)
            for n in range(EARLY_WO, KC):
                if n == 6:
                    dve.wait_ge(o_hi, 1)
                    nc.vector.tensor_tensor(o_part[1][:, 0, LAST, :], o_raw[:, 0, LAST, :],
                                            o_part[0][:, 0, LAST, :].bitcast(F32), ALU.subtract).then_inc(o_lo, 1)
                dve.wait_ge(wo_hi, n + 1)
                nc.vector.tensor_tensor(wo(1, n), S.raw[:, n % 4, :], wo(0, n).bitcast(F32),
                                        ALU.subtract).then_inc(wo_lo, 1)
            dve.wait_ge(ln_in, 32)

            def body(t, par, nth):
                row = x1[:, par, :]
                dve.wait_ge(x_in[par], 16 * nth + 16)
                dve.wait_ge(x1_stored[par], 16 * nth + 16)
                for h in range(2):
                    cols = slice(h * HALF, (h + 1) * HALF)
                    dve.wait_ge(y_full, 2 * t + (h + 1 + 4))
                    nc.vector.scalar_tensor_tensor(out=row[:, cols], in0=xin[:, par, cols], scalar=ALPHA,
                                                   in1=S.ps[2 * par + h][:, :], op0=ALU.mult, op1=ALU.add)\
                        .then_inc(y_free, 1)
                    dve.wait_ge(y_free, 2 * t + (h + 1 + 4))
                    half_statistics(nc, row, stats[:, par], h, chain)
                layer_norm_start(nc, dve, stats[:, par], mv[:, par], chain, LN_STEPS * t)
                layer_norm_finish(nc, dve, row, mv[:, par], gain[:, :], shift[:, :], chain, LN_STEPS * t,
                                  deviation, t + 1, x1_ready)
                if not (isinstance(t, int) and t == 0):
                    turned_tile(t - 1, 1 - par)
                if isinstance(t, int) and t == GROUPS - 1:
                    turned_tile(t, par)

            def turned_tile(t, par):
                for q in range(2):
                    dve.wait_ge(turned_hi, 2 * t + (q + 1))
                    nc.vector.tensor_tensor(S.act[1][:, 4 * q:4 * q + 4, bass.ds(t * P, P)], x1_T_tile(par, q),
                                            S.act[0][:, 4 * q:4 * q + 4, bass.ds(t * P, P)].bitcast(F32),
                                            ALU.subtract).then_inc(turned_lo, 1)

            tiles_loop(dve, body)

        @block.tensor
        def _(pe):
            pe.sem_inc(y_full, 4)

            def turn(t, par):
                for q in range(2):
                    pe.wait_ge(x1_ready, 2 * t + (q + 1))
                    pe.wait_ge(turned_lo, 2 * t + (q + 1))
                    for i in range(4):
                        k = 4 * q + i
                        mm = nc.tensor.transpose(S.ps[4 + 2 * par + q][:, i * P:(i + 1) * P],
                                                 x1[:, par, k * P:(k + 1) * P], S.ident[:, :])
                    mm.then_inc(turned, 1)

            def body(t, par, nth):
                first = isinstance(t, int) and t == 0
                if first:
                    pe.wait_ge(S.first_lo, 1)
                else:
                    pe.wait_ge(o_lo, t + (1 + 2))
                for h in range(2):
                    pe.wait_ge(y_free, 2 * t + (h + 1))
                def products(k, h):
                    for n, (wp, ap) in enumerate(PASSES):
                        tile = first_tile(S, ap)[:, k, :] if first and k < LAST else o_part[ap][:, par, k, :]
                        mm = nc.tensor.matmul(S.ps[2 * par + h][:, :], tile, wo(wp, k)[:, h * HALF:(h + 1) * HALF],
                                              start=(k == 0 and n == 0), stop=(k == KC - 1 and n == 2))
                    if k == KC - 1:
                        mm.then_inc(y_full, 1)

                if first:
                    for k in range(KC):
                        pe.wait_ge(wo_lo, k + 1)
                        if k == LAST:
                            pe.wait_ge(o_lo, 1 + 2)
                        for h in range(2):
                            products(k, h)
                else:
                    for h in range(2):
                        for k in range(KC):
                            products(k, h)
                if not first:
                    turn(t - 1, 1 - par)
                if isinstance(t, int) and t == GROUPS - 1:
                    turn(t, par)

            tiles_loop(pe, body)


BLOCK_CHUNKS = 4
BLOCKS = FF // (BLOCK_CHUNKS * P)


def load_gate(sp, S, w_gate, half, i):
    load_rows(sp, S, i, w_gate, 2 * i * P, 2, HALF, half * HALF).then_inc(S.ff_in[i], 16)


def mlp(nc, S, w_ff1, w_ff2, ln_g, ln_b, w_gate, out):
    with ExitStack() as ctx:
        def sb(name, shape, dt=F32):
            return ctx.enter_context(nc.sbuf_tensor(name, shape, dt))

        def sem(name):
            return ctx.enter_context(nc.semaphore(name))

        y = sb("y", [P, GROUPS, D])
        hid = [sb(f"hidden_T_{n}", [P, BLOCK_CHUNKS, T], F32R) for n in ("hi", "lo")]
        wb = [sb(f"w_ff2_{n}", [P, BLOCK_CHUNKS, D], F32R) for n in ("hi", "lo")]
        w1 = [sb(f"w_ff1_{n}", [P, 2, KC, P], F32R) for n in ("hi", "lo")]
        gated = sb("gated", [P, 2, HALF])
        relu = sb("relu", [P, 2, HALF])
        stats, mv = sb("ln2_stats", [P, 2, 2, 6]), sb("ln2_mean_var", [P, 2, 8])

        y_in = [sem(f"y_in{t}") for t in range(GROUPS)]
        w_hi = sem("mlp_w_hi_done")
        w_lo = sem("mlp_w_lo_done")
        first_gate_hi = sem("first_gate_hi_done")
        first_gate_lo = sem("first_gate_lo_done")
        gate_full = sem("gate_full")
        wg_used = sem("w_gate_chunk_used")
        sigmoid = sem("sigmoid_done")
        product = sem("product_done")
        gate_done = sem("gate_done")
        ff1_full = sem("ff1_full")
        relu_done = sem("relu_done")
        square = sem("square_done")
        hid_hi = sem("hidden_hi_done")
        hid_lo = sem("hidden_lo_done")
        ff2_full = sem("ff2_full")
        y_added = sem("y_added")
        ln_in = sem("ln2_in")
        chain = sem("ln2_chain")
        deviation = sem("ln2_deviation")
        out_ready = sem("out_ready")
        out_stored = sem("out_stored_final")
        block = ctx.enter_context(nc.Block())

        W_BLOCK = 8
        GROUPS1 = 2 * BLOCK_CHUNKS
        TILES2 = 2 * GROUPS

        def gate_columns(part, k):
            return wb[part][:, k // 2, (k % 2) * HALF:(k % 2 + 1) * HALF]

        def embedded(t, cols):
            return hid[t // 4][:, t % 4, cols].bitcast(F32)

        def blocks_loop(eng, body):
            with eng.Fori(0, BLOCKS - 1) as b:
                body(b, False)
            body(BLOCKS - 1, True)

        @block.sync
        def _(sp):
            def value(v):
                return in_register(sp, v)

            def load_ff1(c, column):
                src = bass.AP(w_ff1.tensor, column, [[FF, P], [P * FF, KC], [1, P]])
                sp.dma_start(S.raw[:, c, :].rearrange("p (k n) -> p k n", k=KC), src).then_inc(S.ff_in[c], 16)

            for i in range(2):
                sp.wait_ge(S.x1_stored[i], 16 * (GROUPS // 2 + 1))
            for t in range(GROUPS):
                sp.dma_start(y[:, t, :], S.x1[t]).then_inc(y_in[t], 16)
                sp.dma_start(embedded(t, slice(0, D)), S.embedded[t]).then_inc(y_in[t], 16)
            for i in range(BLOCK_CHUNKS):
                sp.wait_ge(w_lo, i + 1)
                load_gate(sp, S, w_gate, 1, i)
            for c in range(BLOCK_CHUNKS):
                sp.wait_ge(w_lo, 4 + c + 1)
                load_ff1(c, c * P)

            def body(b, last):
                row = value(b * (BLOCK_CHUNKS * P * D))
                for c in range(BLOCK_CHUNKS):
                    place = value(row + c * P * D)
                    split = value(8 * b + (W_BLOCK + c + 1))
                    sp.wait_ge(w_lo, split)
                    sp.dma_start(S.raw[:, c, :], bass.AP(w_ff2.tensor, place, [[D, P], [1, D]]))\
                      .then_inc(S.ff_in[c], 16)
                if last:
                    for c, a in ((0, ln_g), (1, ln_b)):
                        sp.wait_ge(w_lo, 8 * (BLOCKS - 1) + W_BLOCK + 4 + c + 1)
                        sp.dma_start(S.raw[:, c, :], broadcast_row(a)).then_inc(ln_in, 16)
                    return
                for c in range(BLOCK_CHUNKS):
                    place = value(b * (BLOCK_CHUNKS * P) + (BLOCK_CHUNKS + c) * P)
                    split = value(8 * b + (W_BLOCK + 4 + c + 1))
                    sp.wait_ge(w_lo, split)
                    load_ff1(c, place)

            blocks_loop(sp, body)
            for t in range(GROUPS):
                for h in range(2 if t == GROUPS - 1 else 1):
                    cols = slice(h * HALF, (h + 1) * HALF) if t == GROUPS - 1 else slice(0, D)
                    sp.wait_ge(out_ready, 2 * t + h + 1 if t == GROUPS - 1 else 2 * t + 2)
                    sp.dma_start(token_tile(out, t)[:, :, cols], y[:, t, cols]).then_inc(out_stored, 16)
            sp.wait_ge(out_stored, 16 * (GROUPS + 1))

        IN_BLOCK = [("ff1", 2), ("ff1", 3), ("ff2", 0), ("ff2", 1), ("ff2", 2), ("ff2", 3), ("ff1", 4), ("ff1", 5)]
        SPLIT_AFTER = [2, 4, 4, 5, 5, 6, 8, 8]

        def block_target(part, i):
            kind, c = IN_BLOCK[i]
            return (w1[part][:, c % 2, :, :].rearrange("p k n -> p (k n)") if kind == "ff1" else wb[part][:, c, :])

        @block.gpsimd
        def _(pool):
            def low(dst, hi, slot, count):
                pool.wait_ge(w_hi, count)
                nc.gpsimd.tensor_tensor(dst, S.raw[:, slot, :], hi.bitcast(F32), ALU.subtract).then_inc(w_lo, 1)

            pool.wait_ge(w_lo, W_BLOCK)
            for c in range(2):
                low(block_target(1, 6 + c), block_target(0, 6 + c), c, W_BLOCK + c + 1)

            def body(b, last):
                for i in range(GROUPS1 + 1):
                    for s, after in enumerate(SPLIT_AFTER):
                        if after == i and not (last and s >= 6):
                            low(block_target(1, s), block_target(0, s), IN_BLOCK[s][1] % 4, 8 * b + (W_BLOCK + 2 + s + 1))

            blocks_loop(pool, body)

        @block.scalar
        def _(act):
            def high(dst, slot, loads):
                act.wait_ge(S.ff_in[slot], loads)
                nc.scalar.activation(dst, S.raw[:, slot, :], ACT.Copy).then_inc(w_hi, 1)

            act.wait_ge(S.ff_in[0], 16)
            nc.scalar.activation(gate_columns(0, 0), S.raw[:, 0, 0:HALF], ACT.Copy).then_inc(first_gate_hi, 1)
            nc.scalar.activation(gate_columns(0, 1), S.raw[:, 0, HALF:D], ACT.Copy).then_inc(w_hi, 1)
            for i in range(1, 4):
                high(wb[0][:, i, :], i, 16)

            def sigmoids(half, first, last):
                for t in range(first, last):
                    u = GROUPS * half + t
                    act.wait_ge(gate_full, u + 1)
                    act.wait_ge(gate_done, u + 1)
                    nc.scalar.activation(gated[:, u % 2, :], S.ps[4 + u % 2][:, :], ACT.Sigmoid).then_inc(sigmoid, 1)

            sigmoids(0, 0, GROUPS - 1)
            for i in range(4):
                if i < 3:
                    act.wait_ge(wg_used, i + 1)
                else:
                    sigmoids(0, GROUPS - 1, GROUPS)
                high(wb[0][:, i, :], i, 32)
            for c in range(2):
                high(block_target(0, 6 + c), c, 48)
            sigmoids(1, 0, GROUPS)
            act.wait_ge(gate_done, 2 * GROUPS + 2)

            def body(b, last):
                for i in range(GROUPS1 + 1):
                    for s, after in enumerate(SPLIT_AFTER):
                        if after == i and not (last and s >= 6):
                            kind, c = IN_BLOCK[s]
                            if kind == "ff1" and s >= 6:
                                act.wait_ge(ff1_full, GROUPS1 * b + (4 + 2 * (c - 2) + 2))
                            loads = (3 if kind == "ff1" else 4) + (2 if c >= 4 else 0)
                            high(block_target(0, s), c % 4, 32 * b + 16 * loads)
                    if i < GROUPS1:
                        act.wait_ge(ff1_full, GROUPS1 * b + (i + 1 + 4))
                        act.wait_ge(hid_lo, GROUPS1 * b + (i + 1 + 2))
                        nc.scalar.activation(relu[:, i % 2, :], S.ps[i % 4][:, :], ACT.Relu).then_inc(relu_done, 1)
                        act.wait_ge(square, GROUPS1 * b + (i + 1))
                        nc.scalar.activation(hid[0][:, i // 2, (i % 2) * HALF:(i % 2 + 1) * HALF], relu[:, i % 2, :],
                                             ACT.Copy).then_inc(hid_hi, 1)

            blocks_loop(act, body)
            for t in range(GROUPS):
                act.wait_ge(chain, LN_STEPS * t + 4)
                nc.scalar.activation(mv[:, t % 2, 3:4], mv[:, t % 2, 2:3], ACT.Sqrt).then_inc(deviation, 1)

        @block.vector
        def _(dve):
            for credit, n in ((gate_done, 2), (hid_lo, 4), (y_added, 4)):
                dve.sem_inc(credit, n)

            def low(m):
                dve.wait_ge(w_hi, m + 1)
                nc.vector.tensor_tensor(wb[1][:, m % 4, :], S.raw[:, m % 4, :], wb[0][:, m % 4, :].bitcast(F32),
                                        ALU.subtract).then_inc(w_lo, 1)

            dve.wait_ge(first_gate_hi, 1)
            nc.vector.tensor_tensor(gate_columns(1, 0), S.raw[:, 0, 0:HALF], gate_columns(0, 0).bitcast(F32),
                                    ALU.subtract).then_inc(first_gate_lo, 1)
            dve.wait_ge(w_hi, 1)
            nc.vector.tensor_tensor(gate_columns(1, 1), S.raw[:, 0, HALF:D], gate_columns(0, 1).bitcast(F32),
                                    ALU.subtract).then_inc(w_lo, 1)
            for m in range(1, 4):
                low(m)
            for u in range(2 * GROUPS):
                half, t = divmod(u, GROUPS)
                cols = slice(half * HALF, (half + 1) * HALF)
                dve.wait_ge(sigmoid, u + 1)
                dve.wait_ge(y_in[t], 32)
                nc.vector.tensor_tensor(gated[:, u % 2, :], gated[:, u % 2, :], embedded(t, cols), ALU.mult)\
                    .then_inc(product, 1)
                dve.wait_ge(product, u + 1)
                nc.vector.scalar_tensor_tensor(out=y[:, t, cols], in0=y[:, t, cols], scalar=ALPHA,
                                               in1=gated[:, u % 2, :], op0=ALU.mult, op1=ALU.add)\
                    .then_inc(gate_done, 1)
                if u == GROUPS - 2:
                    for m in range(4, 7):
                        low(m)
                if u == GROUPS - 1:
                    low(7)

            def body(b, last):
                for i in range(GROUPS1):
                    dve.wait_ge(relu_done, GROUPS1 * b + (i + 1))
                    nc.vector.tensor_tensor(relu[:, i % 2, :], relu[:, i % 2, :], relu[:, i % 2, :], ALU.mult)\
                        .then_inc(square, 1)
                    dve.wait_ge(hid_hi, GROUPS1 * b + (i + 1))
                    cols = slice((i % 2) * HALF, (i % 2 + 1) * HALF)
                    nc.vector.tensor_tensor(hid[1][:, i // 2, cols], relu[:, i % 2, :],
                                            hid[0][:, i // 2, cols].bitcast(F32), ALU.subtract).then_inc(hid_lo, 1)
                for n in range(TILES2):
                    t, h = divmod(n, 2)
                    cols = slice(h * HALF, (h + 1) * HALF)
                    dve.wait_ge(ff2_full, TILES2 * b + (n + 1))
                    nc.vector.tensor_tensor(y[:, t, cols], y[:, t, cols], S.ps[4 + n % 4][:, :], ALU.add)\
                        .then_inc(y_added, 1)
                    if last:
                        dve.wait_ge(y_added, TILES2 * b + (n + 1 + 4))
                        half_statistics(nc, y[:, t, :], stats[:, t % 2], h, chain)
                    if last and h == 1:
                        if t == 0:
                            dve.wait_ge(ln_in, 32)
                        layer_norm_start(nc, dve, stats[:, t % 2], mv[:, t % 2], chain, LN_STEPS * t)
                        layer_norm_finish(nc, dve, y[:, t, :], mv[:, t % 2], S.raw[:, 0, :], S.raw[:, 1, :], chain,
                                          LN_STEPS * t, deviation, t + 1, out_ready)

            blocks_loop(dve, body)

        @block.tensor
        def _(pe):
            pe.sem_inc(ff1_full, 4)
            def gate(u):
                half, t = divmod(u, GROUPS)
                pe.wait_ge(gate_done, u + 1)
                for k in range(KC):
                    if u == 0 and k < 2:
                        pe.wait_ge(*((first_gate_lo, 1), (w_lo, 1))[k])
                    elif t == 0 and k % 2 == 0:
                        pe.wait_ge(w_lo, 4 * half + k // 2 + 1)
                    for n, (wp, ap) in enumerate(PASSES):
                        mm = nc.tensor.matmul(S.ps[4 + u % 2][:, :], S.act[ap][:, k, t * P:(t + 1) * P],
                                              gate_columns(wp, k), start=(k == 0 and n == 0),
                                              stop=(k == KC - 1 and n == 2))
                    if u == GROUPS - 1 and k % 2 and k < KC - 1:
                        mm.then_inc(wg_used, 1)
                mm.then_inc(gate_full, 1)

            for u in range(2 * GROUPS):
                gate(u)

            def body(b, last):
                for i in range(GROUPS1):
                    c, th = divmod(i, 2)
                    if th == 0:
                        pe.wait_ge(w_lo, 8 * b + (W_BLOCK + c + 1))
                    pe.wait_ge(hid_lo, GROUPS1 * b + (i + 1))
                    for k in range(KC):
                        for n, (wp, ap) in enumerate(PASSES):
                            mm = nc.tensor.matmul(S.ps[i % 4][:, :], w1[wp][:, c % 2, k, :],
                                                  S.act[ap][:, k, th * HALF:(th + 1) * HALF],
                                                  start=(k == 0 and n == 0), stop=(k == KC - 1 and n == 2))
                    mm.then_inc(ff1_full, 1)
                for n in range(TILES2):
                    t, h = divmod(n, 2)
                    if n == 0:
                        pe.wait_ge(w_lo, 8 * b + (W_BLOCK + 8))
                    if n in (0, TILES2 // 2):
                        pe.wait_ge(hid_lo, GROUPS1 * b + (GROUPS1 - 1 + (n > 0) + 4))
                    pe.wait_ge(y_added, TILES2 * b + (n + 1))
                    for k in range(BLOCK_CHUNKS):
                        for i, (wp, ap) in enumerate(PASSES):
                            mm = nc.tensor.matmul(S.ps[4 + n % 4][:, :], hid[ap][:, k, t * P:(t + 1) * P],
                                                  wb[wp][:, k, h * HALF:(h + 1) * HALF],
                                                  start=(k == 0 and i == 0), stop=(k == BLOCK_CHUNKS - 1 and i == 2))
                    mm.then_inc(ff2_full, 1)

            blocks_loop(pe, body)


INPUTS = ["x", "p", "na_w_qkv", "na_rpb", "na_w_o", "ln1_g", "ln1_b", "w_ff1", "w_ff2", "ln2_g", "ln2_b",
          "w_ple_gate", "w_ple_proj"]


def column_mask():
    query = np.arange(P) % GC
    key = np.arange(3 * GC).reshape(3, 1, GC)
    inside = (key[None] >= query[:, None, None, None]) & (key[None] < query[:, None, None, None] + KW)
    return np.broadcast_to(np.where(inside, 0.0, MASKED), (P, 3, ROWS, GC)).reshape(P, NB).astype(np.float32)


def kernel(**inputs):
    import concourse.bacc as bacc
    from concourse.bass_utils import run_bass_kernel_spmd

    nc = bacc.Bacc("TRN2", target_bir_lowering=False, num_devices=1)
    arrays = {f"in_{name}": np.ascontiguousarray(inputs[name]) for name in INPUTS}
    arrays["column_mask_table"] = column_mask()
    args = [nc.dram_tensor(name, a.shape, mybir.dt.from_np(a.dtype), kind="ExternalInput").ap()
            for name, a in arrays.items()]
    shape = inputs["x"].shape
    args.append(nc.dram_tensor("out", shape, F32, kind="ExternalOutput").ap())
    build_program(nc, *args)
    result = run_bass_kernel_spmd(nc, [arrays], core_ids=[0])
    return result.results[0]["out"]
```
